# Optimizing a Trainium2 kernel written in Bass

```python
import jax, jax.numpy as jnp
from jax import lax
import numpy as np

D_MODEL = 1024
BATCH = 1
SEQ = 1024
DEPTH = 1

D_MIX = D_MODEL
D_ATT = D_MIX // 2
D_CONV = D_MIX - D_ATT
HEAD_DIM = 64
N_HEADS = D_ATT // HEAD_DIM
N_IDX_HEADS = 4
IDX_DIM = 64
TOPK_MAX = 256
CONV_WIDTH = 31
Q_BLOCK = 128
EPS = 1e-6
NEG = -1e30

IN_WIDTHS = (D_ATT, HEAD_DIM, HEAD_DIM, D_ATT, N_IDX_HEADS * IDX_DIM, IDX_DIM, N_IDX_HEADS, 2 * D_CONV, D_CONV)
D_IN = sum(IN_WIDTHS)
SPLIT_POINTS = tuple(int(p) for p in np.cumsum(IN_WIDTHS)[:-1])

kernel_name = "hybrid_dsa_conformer_conv_block"

def rmsnorm(x, g):
    xf = x.astype(jnp.float32)
    y = xf * lax.rsqrt(jnp.mean(xf * xf, axis=-1, keepdims=True) + EPS)
    return (y * g.astype(jnp.float32)).astype(x.dtype)

def layernorm(x, g, b):
    xf = x.astype(jnp.float32)
    mu = jnp.mean(xf, axis=-1, keepdims=True)
    var = jnp.mean(jnp.square(xf - mu), axis=-1, keepdims=True)
    y = (xf - mu) * lax.rsqrt(var + EPS)
    return (y * g.astype(jnp.float32) + b.astype(jnp.float32)).astype(x.dtype)

def alibi_slopes(n_heads):
    h = jnp.arange(1, n_heads + 1, dtype=jnp.float32)
    return jnp.exp2(-8.0 * h / n_heads)

def dsa_sparse_attention(q, k, v, q_idx, k_idx, w_idx):
    B, S = q.shape[0], q.shape[1]
    top_k = min(TOPK_MAX, S // 4)
    n_blocks = S // Q_BLOCK
    slopes = alibi_slopes(N_HEADS)
    key_pos = jnp.arange(S, dtype=jnp.int32)
    k_idx_f = k_idx.astype(jnp.float32)
    gather = jax.vmap(lambda arr, ids: arr[ids])

    def one_block(i):
        t0 = i * Q_BLOCK
        qb = lax.dynamic_slice_in_dim(q, t0, Q_BLOCK, axis=1)
        qib = lax.dynamic_slice_in_dim(q_idx, t0, Q_BLOCK, axis=1)
        wib = lax.dynamic_slice_in_dim(w_idx, t0, Q_BLOCK, axis=1)
        t_pos = t0 + jnp.arange(Q_BLOCK, dtype=jnp.int32)
        causal = key_pos[None, :] <= t_pos[:, None]
        logits = jnp.einsum('bthd,bsd->bths', qib.astype(jnp.float32), k_idx_f)
        iscore = jnp.einsum('bth,bths->bts', wib.astype(jnp.float32), jax.nn.relu(logits))
        iscore = jnp.where(causal[None], iscore, NEG)
        _, sel = lax.top_k(iscore, top_k)
        k_sel = gather(k, sel).astype(jnp.float32)
        v_sel = gather(v, sel).astype(jnp.float32)
        s = jnp.einsum('bthd,btkd->bhtk', qb.astype(jnp.float32), k_sel) * (HEAD_DIM ** -0.5)
        dist = (t_pos[None, :, None] - sel).astype(jnp.float32)
        s = s - slopes[None, :, None, None] * dist[:, None]
        valid = sel <= t_pos[None, :, None]
        s = jnp.where(valid[:, None], s, NEG)
        p = jax.nn.softmax(s, axis=-1)
        o = jnp.einsum('bhtk,btkd->bthd', p, v_sel)
        return o.astype(q.dtype)

    out = lax.map(one_block, jnp.arange(n_blocks))
    return out.transpose(1, 0, 2, 3, 4).reshape(B, S, N_HEADS * HEAD_DIM)

def conformer_conv(u_glu, w_dw, b_dw, g_n, b_n, w_pw2, b_pw2):
    a, g = jnp.split(u_glu, 2, axis=-1)
    u = a * jax.nn.sigmoid(g)
    u_pad = jnp.pad(u, ((0, 0), (CONV_WIDTH - 1, 0), (0, 0)))
    y = lax.conv_general_dilated(
        u_pad, w_dw[:, None, :].astype(u.dtype), window_strides=(1,), padding='VALID',
        dimension_numbers=('NWC', 'WIO', 'NWC'), feature_group_count=D_CONV) + b_dw
    y = jax.nn.silu(layernorm(y, g_n, b_n))
    return y @ w_pw2 + b_pw2

def setup_inputs(seed: int = 0) -> dict:
    key = jax.random.key(seed)
    ks = jax.random.split(key, 16)
    nrm = jax.random.normal
    f32 = jnp.float32
    return {
        "x": nrm(ks[0], (BATCH, SEQ, D_MODEL), f32),
        "c": nrm(ks[1], (BATCH, D_MODEL), f32),
        "w_ada": nrm(ks[2], (DEPTH, D_MODEL, 3 * D_MODEL), f32) * (0.5 * D_MODEL ** -0.5),
        "b_ada": nrm(ks[3], (DEPTH, 3 * D_MODEL), f32) * 0.02,
        "g_pre": 1.0 + 0.1 * nrm(ks[4], (DEPTH, D_MODEL), f32),
        "w_in": nrm(ks[5], (DEPTH, D_MODEL, D_IN), f32) * (D_MODEL ** -0.5),
        "w_dw": nrm(ks[6], (DEPTH, CONV_WIDTH, D_CONV), f32) * (CONV_WIDTH ** -0.5),
        "b_dw": nrm(ks[7], (DEPTH, D_CONV), f32) * 0.02,
        "g_cnorm": 1.0 + 0.1 * nrm(ks[8], (DEPTH, D_CONV), f32),
        "b_cnorm": nrm(ks[9], (DEPTH, D_CONV), f32) * 0.02,
        "w_pw2": nrm(ks[10], (DEPTH, D_CONV, D_CONV), f32) * (D_CONV ** -0.5),
        "b_pw2": nrm(ks[11], (DEPTH, D_CONV), f32) * 0.02,
        "w_out": nrm(ks[12], (DEPTH, D_MIX, D_MODEL), f32) * (D_MIX ** -0.5),
        "g_post": 1.0 + 0.1 * nrm(ks[13], (DEPTH, D_MODEL), f32),
    }

def reference(x, c, w_ada, b_ada, g_pre, w_in, w_dw, b_dw, g_cnorm, b_cnorm, w_pw2, b_pw2, w_out, g_post):
    B, S, _ = x.shape
    c_act = jax.nn.silu(c)
    for l in range(DEPTH):
        mod = c_act @ w_ada[l] + b_ada[l]
        shift, scale, gate = jnp.split(mod, 3, axis=-1)
        h = rmsnorm(x, g_pre[l]) * (1.0 + scale[:, None, :]) + shift[:, None, :]
        proj = h @ w_in[l]
        q, k, v, g_att, q_i, k_i, w_i, u_glu, g_conv = jnp.split(proj, SPLIT_POINTS, axis=-1)
        q = q.reshape(B, S, N_HEADS, HEAD_DIM)
        q_i = q_i.reshape(B, S, N_IDX_HEADS, IDX_DIM)
        y_att = dsa_sparse_attention(q, k, v, q_i, k_i, w_i) * jax.nn.silu(g_att)
        y_conv = conformer_conv(u_glu, w_dw[l], b_dw[l], g_cnorm[l], b_cnorm[l], w_pw2[l], b_pw2[l]) * jax.nn.silu(g_conv)
        y = jnp.concatenate([y_att, y_conv], axis=-1) @ w_out[l]
        x = x + gate[:, None, :] * rmsnorm(y, g_post[l])
    return x


_drawn_inputs = setup_inputs


def setup_inputs(seed=0):
    import zlib

    import numpy as np

    out = dict(_drawn_inputs(seed))
    spreads = {}
    factors = {'b_dw': 7.373, 'b_cnorm': 8.0, 'b_pw2': 7.541}
    for name, (base, spread) in spreads.items():
        noise = np.random.default_rng([zlib.crc32(name.encode()), seed]).standard_normal(out[name].shape)
        drawn = base * np.exp(spread * noise) if base else spread * noise
        out[name] = __import__('jax').numpy.asarray(drawn.astype(out[name].dtype))
    for name, factor in factors.items():
        out[name] = (out[name] * factor).astype(out[name].dtype)
    return out
```

```python
from contextlib import ExitStack

import concourse.bass as bass
from concourse import mybir

ALU = mybir.AluOpType
ACT = mybir.ActivationFunctionType
F32 = mybir.dt.float32
F32R = mybir.dt.float32r
F16 = mybir.dt.float16
BF16 = mybir.dt.bfloat16
I32 = mybir.dt.int32

P = 128
T = 1024
D = 1024
TT = T // P
KC = D // P
HALF = 512
HD = 64
NH = 8
NI = 4
TOPK = 256
TAPS = 31
PAD = TAPS - 1
CC = 4
EPS = 1e-6
NEG = -1e30
FIRST = TOPK // P

CHUNKS = ["KI", "QI0", "QI1", "G0", "A0", "G1", "A1", "KV", "Q0", "G2", "A2", "Q1", "Q2",
          "G3", "A3", "Q3", "GA0", "GA1", "GA2", "GA3", "GC0", "GC1", "GC2", "GC3"]
AT = {name: n for n, name in enumerate(CHUNKS)}
NCH = len(CHUNKS)


def bank_plan():
    out, n = [], 0
    while n < NCH:
        if CHUNKS[n][0] == "G" and CHUNKS[n][1].isdigit():
            out += [(n, 0), (n + 1, 0), (n, 1), (n + 1, 1)]
            n += 2
        else:
            out += [(n, 0), (n, 1)]
            n += 1
    return out


BANKS = bank_plan()
EARLY = 10
DURING = 40
GATES = 32
LAST_OF = {c: max(b for b, (x, _) in enumerate(BANKS) if x == c) for c in range(NCH)}
BANK_OF = {x: b for b, x in enumerate(BANKS)}

GROUPS = [(2, 3, 7), (4, 5, 6)]
ORDER = [i for g in GROUPS for i in g]
COL = {i: n for n, i in enumerate(ORDER)}
ROUNDS = 32


def keys(i):
    return (i + 1) * P


def off(i):
    return P * i * (i + 1) // 2


NSMALL = 184
XW = off(TT)
RW = T + 7 * P

COLS, _n = {}, 0
for _name, _w in (("c", KC), ("b_ada", 3 * KC), ("g_pre", KC), ("g_post", KC), ("w_dw", CC * TAPS), ("b_dw", CC),
                  ("g_cn", CC), ("b_cn", CC), ("b_pw2", CC)):
    COLS[_name] = (_n, _w)
    _n += _w
NCOLS = _n
CONS, _n = {}, 0
for _name, _w in (("ident", P), ("mean", P), ("qscale", CC), ("few", 6), ("eps", 1)):
    CONS[_name] = (_n, _w)
    _n += _w
NCONS = _n


def hybrid_block(nc, x, cols, consts, masks, dist, w_ada, w_in, w_pw2, w_out, out):
    with ExitStack() as ctx:
        nc_base = 16512
        top = 229344

        def at(name, kb, shape, dt=F32):
            size = 1
            for s in shape[1:]:
                size *= s
            size *= 2 if dt in (F16, BF16) else 4
            assert nc_base + kb + size <= top, (name, kb, size)
            return nc.alloc_sbuf_tensor_at(name, shape, dt, offset=nc_base + kb)

        K = 1024
        oH, oW = 0, 64 * K
        oY, oQ = oW + 24 * K, oW + 40 * K
        oGA = oQ + 16 * K
        oX = oGA + 16 * K
        oKI = oX + 4 * XW
        oQI = oKI + 8 * K
        oU = oQI + 16 * K
        oR = oU + (8 * (PAD + T) + 31) // 32 * 32
        oV = oR + 4 * K
        oM = oV + 2 * K
        oC = oM + (4 * (NCOLS + 8 + NSMALL) + 31) // 32 * 32
        oT = oC + (4 * (NCONS + ROUNDS + 9) + 31) // 32 * 32
        h_hi = at("h_hi", oH, [P, KC, T], F32R)
        h_lo = at("h_lo", oH + 32 * K, [P, KC, T], F32R)
        z_hi = at("z_hi", oH, [P, CC, T], F32R)
        z_lo = at("z_lo", oH + 16 * K, [P, CC, T], F32R)
        qs = at("qs", oH + 32 * K, [P, NH, T], F32R)
        wo_hi = at("wo_hi", oH, [P, KC, D], F32R)
        wo_lo = at("wo_lo", oY, [P, KC, D], F32R)
        w_raw = at("w_raw", oW, [P, 2, KC, P])
        w_hi = at("w_hi", oW + 8 * K, [P, 2, KC, P], F32R)
        w_lo = at("w_lo", oW + 16 * K, [P, 2, KC, P], F32R)
        sm = at("sm", oW, [P, 2, T])
        pr = at("pr", oW + 8 * K, [P, 2, T])
        pt = at("pt", oW + 16 * K, [P, 2, T])
        ada = at("ada", oY, [P, 4, KC, 256])
        rl = at("rl", oY, [P, 2, T])
        yc = at("yc", oY, [P, CC, T])
        q_raw = at("q_raw", oQ, [P, CC, T])
        ga = at("ga", oGA, [P, CC, T])
        xin = at("xin", oX, [P, TT, D])
        xs = at("xs", oX, [P, XW])
        ki_hi = at("ki_hi", oKI, [P, T], F32R)
        ki_lo = at("ki_lo", oKI + 4 * K, [P, T], F32R)
        k_hi = at("k_hi", oKI, [P, T], F32R)
        k_lo = at("k_lo", oKI + 4 * K, [P, T], F32R)
        qi = at("qi", oQI, [P, NI, T], F32R)
        junk = at("junk", oQI, [P, XW - off(FIRST)], BF16)
        kv_raw = at("kv_raw", oQI + 8448, [P, T])
        gc = at("gc", oQI, [P, CC, T])
        ki_raw = at("ki_raw", oGA + 8 * K, [P, T])
        h32 = at("h32", oGA, [P, 4, HALF])
        u = at("u", oU, [P, 2, PAD + T])
        zt = at("zt", oU, [P, 2, HALF])
        zz = at("zz", oU + 4 * K, [P, 2, HALF])
        wo_raw = at("wo_raw", oU, [P, 2, D])
        yt_hi = at("yt_hi", oU, [P, 2 * CC, P], F32R)
        yt_lo = at("yt_lo", oU + 4 * K, [P, 2 * CC, P], F32R)
        distance = at("distance", oR, [P, RW], F16)
        gate = at("gate", oR, [P, D])
        v = at("v", oV, [P, TT, HD])
        colt = at("colt", oM, [P, NCOLS])
        small = at("small", oM + (4 * NCOLS + 31) // 32 * 32, [P, NSMALL])
        cons = at("cons", oC, [P, NCONS])
        bits = at("bits", oC + (4 * NCONS + 31) // 32 * 32, [P, ROUNDS + 1], I32)
        t_hi = at("t_hi", oT, [P, 2, HALF], F32R)
        t_lo = at("t_lo", oT + 4 * K, [P, 2, HALF], F32R)
        sq = at("sq", oT, [P, 2, HALF])
        rstd = at("rstd", oT + 4 * K, [P, 2, HALF])
        diag = at("diag", oT, [P, KC, P])
        xo = at("xo", oT, [P, 2, D])
        th = at("th", oT + 8 * K, [P, HALF])
        tg = at("tg", oT + 10 * K, [P, HALF])
        o_sb = at("o_sb", oT + 8 * K, [P, CC * P])
        sq_junk = at("sq_junk", oT + 10 * K, [P, D], BF16)
        q_lo = at("q_lo", oQ, [P, CC, T], F32R)
        x_sq = at("x_sq", oH, [P, D])
        tie = at("tie", oW, [P, T])
        run = at("run", oW + 4 * K, [P, T])

        psum = ctx.enter_context(nc.psum_tensor("psum", [P, 8, HALF], F32))

        _c = {}

        def col(name, j=0, n=1):
            a, w = COLS[name]
            return colt[:, a + j:a + j + n]

        def con(name, j=0, n=None):
            a, w = CONS[name]
            return cons[:, a + j:a + (w if n is None else j + n)]

        used = [0]

        def scratch(n):
            used[0] += n
            assert used[0] <= NSMALL
            return small[:, used[0] - n:used[0]]

        ss, ms, rx, pw = scratch(TT), scratch(TT), scratch(TT), scratch(TT)
        c_th, c_act = scratch(KC), scratch(KC)
        mod, g1 = scratch(3 * KC), scratch(KC)
        found_f, cand_f, sums, cond_f, f_tmp = scratch(6), scratch(6), scratch(6), scratch(6), scratch(6)
        found, cand, cond, itmp = (a.bitcast(I32) for a in (found_f, cand_f, cond_f, f_tmp))
        above = scratch(6)
        wi = scratch(TT * NI)
        mx, nb = scratch(2), scratch(2)
        denom = scratch(2 * NH)
        rden = scratch(NH)

        def sem(name):
            return ctx.enter_context(nc.semaphore(name))

        s_tables = sem("tables_loaded")
        s_x = [sem(f"x_loaded_{i}") for i in range(TT)]
        s_ada = [sem(f"ada_loaded_{i}") for i in range(4)]
        s_w = [sem(f"w_loaded_{i}") for i in range(2)]
        s_dup = sem("ki_doubled")
        s_kdup = sem("k_doubled")
        s_qst = [sem(f"qi_stacked_{i}") for i in range(2)]
        s_qs = sem("q_stacked")
        s_wo = [sem(f"wo_loaded_{i}") for i in range(2)]
        s_xo = [sem(f"x_again_{i}") for i in range(2)]
        s_out = [sem(f"out_stored_{i}") for i in range(2)]
        s_cth = sem("c_tanh_done")
        s_cact = sem("c_act_done")
        s_ss = sem("x_squares_done")
        s_rx = sem("x_rstd_done")
        s_xn = sem("x_normed")
        s_pool = sem("pool_chain")
        s_dve = sem("dve_chain")
        s_mod = sem("mod_columns_done")
        s_g1 = sem("mod_ready")
        s_xt = sem("x_transposed")
        s_h32 = sem("h32_ready")
        s_hhi = sem("h_hi_ready")
        s_hlo = sem("h_lo_ready")
        s_split = sem("w_split")
        s_proj = sem("proj_bank_done")
        s_raw = sem("raw_evacuated")
        s_kihi = sem("ki_hi_ready")
        s_kilo = sem("ki_lo_ready")
        s_thi = sem("t_hi_ready")
        s_tlo = sem("t_lo_ready")
        s_tanh = sem("tanh_ready")
        s_u = sem("u_half_ready")
        s_wit = sem("wi_transposed")
        s_wi = sem("wi_ready")
        s_idx = sem("index_logits_done")
        s_relu = sem("relu_done")
        s_acc = sem("index_score_added")
        s_caus = sem("causal_filled")
        s_cand = [sem(f"candidates_ready_{g}") for g in range(2)]
        s_cnt = [sem(f"counts_ready_{g}") for g in range(2)]
        s_gat = sem("gate_tanh_ready")
        s_silu = sem("gate_silu_ready")
        s_vt = sem("v_transposed")
        s_v = sem("v_ready")
        s_khi = sem("k_hi_ready")
        s_klo = sem("k_lo_ready")
        s_q = sem("q_raw_ready")
        s_y = sem("conv_done")
        s_mu = sem("mean_done")
        s_yc = sem("centred")
        s_sq = sem("square_done")
        s_var = sem("variance_done")
        s_std = sem("std_ready")
        s_yn = sem("normed")
        s_zt = sem("z_affine_tanh_ready")
        s_zs = sem("z_silu_ready")
        s_zhi = sem("z_hi_ready")
        s_zlo = sem("z_lo_ready")
        s_yconv = sem("conv_branch_ready")
        s_qhi = sem("q_hi_ready")
        s_qlo = sem("q_lo_ready")
        s_sel = sem("selection_ready")
        s_bias = sem("bias_ready")
        s_diag = sem("gate_diagonal_ready")
        s_gb = sem("gate_broadcast")
        s_gate = sem("gate_rows_ready")
        s_wos = sem("wo_split")
        s_sc = sem("scores_done")
        s_mx = sem("row_max_ready")
        s_exp = sem("probs_ready")
        s_pt = sem("probs_transposed")
        s_pe0 = [sem("pt_copied_by_act"), sem("pt_copied_by_dve")]
        s_pv = sem("pv_done")
        s_o = sem("o_normalised")
        s_ot = sem("o_transposed")
        s_ya = sem("y_att_ready")
        s_yhi = sem("y_hi_ready")
        s_ylo = sem("y_lo_ready")
        s_op = sem("out_product_done")
        s_osq = sem("out_squares_done")
        s_or = sem("out_rstd_ready")
        s_of = sem("out_tile_ready")

        osq, orr = ss, rx

        def emptied(eng, b):
            if b < 0:
                eng.wait_ge(s_h32, 16 + b + 1)
                return
            if b >= 2 * NCH:
                eng.wait_ge(s_yconv, b - 2 * NCH + 1)
                return
            kind = CHUNKS[BANKS[b][0]]
            same = [x for x in range(b + 1) if CHUNKS[BANKS[x][0]].rstrip("0123456789") == kind.rstrip("0123456789")]
            if kind == "KI":
                eng.wait_ge(s_raw, len(same))
            elif kind == "KV":
                eng.wait_ge(s_raw, 2 + len(same))
            elif kind[:2] == "QI":
                eng.wait_ge(s_tlo, len(same))
            elif kind[0] == "Q":
                eng.wait_ge(s_q, len(same))
            elif kind[:2] in ("GA", "GC"):
                eng.wait_ge(s_gat, b - GATES + 1)
            elif kind[0] == "G":
                eng.wait_ge(s_tanh, len(same))
            else:
                eng.wait_ge(s_u, len(same))

        IDX = [(i, j) for i in range(FIRST, TT) for j in range(NI)]
        UNITS = []
        for i in range(TT):
            for h in range(NH):
                if h == 4 and i >= 1:
                    UNITS.append(("o", i - 1))
                UNITS.append(("h", i, h))
        UNITS.append(("o", TT - 1))
        HEADS = [x for x in UNITS if x[0] == "h"]
        GROUP = [(n, g) for n, (_, i, h) in enumerate(HEADS) for g in range((i + 4) // 4)]
        OWNER = [q % 2 for q in range(len(GROUP))]
        DONE_BY = [sum(1 for p in range(q + 1) if OWNER[p] == OWNER[q]) for q in range(len(GROUP))]
        FIRST_GROUP = {n: min(q for q, (m, _) in enumerate(GROUP) if m == n) for n in range(len(HEADS))}
        LAST_GROUP = {n: max(q for q, (m, _) in enumerate(GROUP) if m == n) for n in range(len(HEADS))}

        def copied(eng, q):
            eng.wait_ge(s_pe0[OWNER[q]], DONE_BY[q])

        block = ctx.enter_context(nc.Block())

        def words(a):
            return a.bitcast(F32)

        @block.sync
        def _(sp):
            def store(i):
                sp.wait_ge(s_of, i + 1)
                sp.dma_start(out[i * P:(i + 1) * P, :], xo[:, i % 2, :]).then_inc(s_out[i % 2], 16)

            sp.dma_start(cons[:], consts).then_inc(s_tables, 16)
            sp.dma_start(bits[:], masks).then_inc(s_tables, 16)
            sp.dma_start(colt[:], cols).then_inc(s_tables, 16)
            sp.dma_start(distance[:], dist).then_inc(s_tables, 16)
            for i in range(TT):
                sp.dma_start(xin[:, i, :], x[i * P:(i + 1) * P, :]).then_inc(s_x[i], 16)

            def load_ada(b):
                if b >= 4:
                    sp.wait_ge(s_mod, b - 3)
                sp.dma_start(ada[:, b % 4], w_ada[b]).then_inc(s_ada[b % 4], 16)

            def load_w(c):
                if c >= 2:
                    sp.wait_ge(s_split, c - 1)
                if c < NCH:
                    sp.dma_start(w_raw[:, c % 2], w_in[c]).then_inc(s_w[c % 2], 16)
                else:
                    sp.dma_start(w_raw[:, c % 2, 0:CC, :], w_pw2[c - NCH]).then_inc(s_w[c % 2], 16)

            def stack_qi(m):
                c, half, s = m // 2, m % 2, m % 2
                sl = slice(half * HALF, (half + 1) * HALF)
                sp.wait_ge(s_tlo, m + 1)
                for head, a in ((2 * c, 0), (2 * c + 1, HD)):
                    sp.dma_start(words(qi[0:HD, head, sl]), words(t_hi[a:a + HD, s, :])).then_inc(s_qst[s], 16)
                    sp.dma_start(words(qi[HD:P, head, sl]), words(t_lo[a:a + HD, s, :])).then_inc(s_qst[s], 16)

            for b in range(8):
                load_ada(b)
            load_w(0)
            load_w(1)
            for b in range(8, 12):
                load_ada(b)
            load_w(2)
            load_w(3)
            sp.wait_ge(s_kilo, 1)
            sp.dma_start(words(ki_hi[HD:P, :]), words(ki_hi[0:HD, :])).then_inc(s_dup, 16)
            sp.dma_start(words(ki_lo[HD:P, :]), words(ki_lo[0:HD, :])).then_inc(s_dup, 16)
            stack_qi(0)
            stack_qi(1)
            load_w(4)
            stack_qi(2)
            stack_qi(3)
            for c in range(5, 10):
                load_w(c)
            sp.wait_ge(s_klo, 1)
            sp.dma_start(words(k_hi[HD:P, :]), words(k_hi[0:HD, :])).then_inc(s_kdup, 16)
            sp.dma_start(words(k_lo[HD:P, :]), words(k_lo[0:HD, :])).then_inc(s_kdup, 16)
            for c in range(10, NCH + CC):
                load_w(c)
            for j in range(CC):
                sp.wait_ge(s_qlo, j + 1)
                sp.dma_start(words(qs[HD:P, 2 * j, :]), words(q_lo[0:HD, j, :])).then_inc(s_qs, 16)
                sp.dma_start(words(qs[0:HD, 2 * j + 1, :]), words(q_lo[HD:P, j, :])).then_inc(s_qs, 16)
            sp.wait_ge(s_zlo, 2 * CC)
            for c in range(KC):
                if c >= 2:
                    sp.wait_ge(s_wos, c - 1)
                sp.dma_start(wo_raw[:, c % 2, :], w_out[c * P:(c + 1) * P, :]).then_inc(s_wo[c % 2], 16)
            sp.wait_ge(s_gb, 1)
            for i in range(TT):
                if i >= 2:
                    sp.wait_ge(s_out[i % 2], 16 * (i // 2))
                sp.dma_start(xo[:, i % 2, :], x[i * P:(i + 1) * P, :]).then_inc(s_xo[i % 2], 16)
                if i >= 1:
                    store(i - 1)
            store(TT - 1)
            for k in range(2):
                sp.wait_ge(s_out[k], 16 * (TT // 2))

        @block.tensor
        def _(pe):
            ident = con("ident")

            def ada_block(b):
                pe.wait_ge(s_ada[b % 4], 16 * (b // 4 + 1))
                for j in range(2):
                    m = 2 * b + j
                    for k in range(KC):
                        last = nc.tensor.matmul(psum[:, 7, m:m + 1], ada[:, b % 4, k, j * P:(j + 1) * P],
                                                c_act[:, k:k + 1], start=(k == 0), stop=(k == KC - 1))
                last.then_inc(s_mod, 1)

            pe.wait_ge(s_cact, 1)
            for b in range(8):
                ada_block(b)
            for t in range(16):
                half, k = t // KC, t % KC
                pe.wait_ge(s_xn, 4 * (half + 1))
                if t >= 4:
                    pe.wait_ge(s_h32, t - 3)
                for j in range(4):
                    last = nc.tensor.transpose(psum[:, t % 4, j * P:(j + 1) * P],
                                               xin[:, 4 * half + j, k * P:(k + 1) * P], ident)
                last.then_inc(s_xt, 1)

            def project(b):
                c, half = BANKS[b]
                sl = slice(half * HALF, (half + 1) * HALF)
                emptied(pe, b - 4)
                pe.wait_ge(s_split, c + 1)
                if b < 2:
                    pe.wait_ge(s_hlo, KC * (half + 1))
                for k in range(KC):
                    for n, (w, h) in enumerate(((w_hi, h_hi), (w_hi, h_lo), (w_lo, h_hi))):
                        last = nc.tensor.matmul(psum[:, b % 4, :], w[:, c % 2, k, :], h[:, k, sl],
                                                start=(k == 0 and n == 0), stop=(k == KC - 1 and n == 2))
                last.then_inc(s_proj, 1)

            for b in range(4):
                project(b)
            pe.wait_ge(s_g1, 1)
            for b in range(8, 12):
                ada_block(b)
            for b in range(4, EARLY):
                project(b)
            pe.wait_ge(s_raw, 2)
            for i in range(TT):
                last = nc.tensor.transpose(psum[:, 4 + i // 4, (i % 4) * P:(i % 4 + 1) * P],
                                           ki_raw[:, i * P:(i + 1) * P], ident)
            last.then_inc(s_wit, 1)
            pe.wait_ge(s_dup, 32)
            for k in range(2):
                pe.wait_ge(s_qst[k], 128)
            for e, (i, j) in enumerate(IDX):
                if e == 0:
                    pe.wait_ge(s_wi, 1)
                if e >= 2:
                    pe.wait_ge(s_relu, e - 1)
                for a in range(0, keys(i), HALF):
                    z = min(a + HALF, keys(i))
                    for n, kk in enumerate((ki_hi, ki_lo)):
                        last = nc.tensor.matmul(psum[:, 4 + 2 * (e % 2) + a // HALF, 0:z - a],
                                                qi[:, j, i * P:(i + 1) * P], kk[:, a:z],
                                                start=(n == 0), stop=(n == 1))
                last.then_inc(s_idx, 1)
            for b in range(EARLY, 18):
                project(b)
            pe.wait_ge(s_raw, 4)
            pe.wait_ge(s_relu, len(IDX))
            for i in range(TT):
                last = nc.tensor.transpose(psum[:, 4 + i // 4, (i % 4) * P:(i % 4 + 1) * P],
                                           kv_raw[:, i * P:(i + 1) * P], ident)
            last.then_inc(s_vt, 1)

            def mean(half):
                pe.wait_ge(s_y, CC * TAPS)
                if half == 0:
                    pe.wait_ge(s_v, 1)
                for c in range(CC):
                    last = nc.tensor.matmul(psum[:, 4 + half, :], con("mean"),
                                            yc[:, c, half * HALF:(half + 1) * HALF], start=(c == 0), stop=(c == CC - 1))
                last.then_inc(s_mu, 1)

            def variance(half):
                for c in range(CC):
                    m = CC * half + c
                    pe.wait_ge(s_sq, m + 1)
                    nc.tensor.matmul(psum[:, 6 + half, :], con("mean"), sq[:, m % 2, :],
                                     start=(c == 0), stop=(c == CC - 1)).then_inc(s_var, 1)

            for b in range(18, DURING + 4):
                project(b)
            mean(0)
            mean(1)
            project(44)
            project(45)
            variance(0)
            project(46)
            variance(1)
            project(47)
            for m in range(CC):
                for half in range(2):
                    b = 48 + 2 * m + half
                    emptied(pe, b - 4)
                    pe.wait_ge(s_split, NCH + m + 1)
                    pe.wait_ge(s_zlo, CC * (half + 1))
                    for k in range(CC):
                        for n, (w, z) in enumerate(((w_hi, z_hi), (w_hi, z_lo), (w_lo, z_hi))):
                            last = nc.tensor.matmul(psum[:, b % 4, :], w[:, (NCH + m) % 2, k, :],
                                                    z[:, k, half * HALF:(half + 1) * HALF],
                                                    start=(k == 0 and n == 0), stop=(k == CC - 1 and n == 2))
                    last.then_inc(s_proj, 1)
            pe.wait_ge(s_diag, 1)
            pe.wait_ge(s_std, 2)
            for k in range(KC):
                last = nc.tensor.matmul(psum[:, 4 + k // 4, (k % 4) * P:(k % 4 + 1) * P], con("mean"), diag[:, k, :],
                                        start=True, stop=True)
            last.then_inc(s_gb, 1)

            pe.wait_ge(s_qs, 32 * CC)
            pe.wait_ge(s_kdup, 32)
            pe.wait_ge(s_gate, 1)

            def free_ring(un):
                if un >= 2:
                    prev = UNITS[un - 2]
                    if prev[0] == "h":
                        pe.wait_ge(s_mx, HEADS.index(prev) + 1)
                    else:
                        pe.wait_ge(s_of, prev[1] + 1)

            def scores(un, i, h):
                free_ring(un)
                for a in range(0, keys(i), HALF):
                    z = min(a + HALF, keys(i))
                    for n, kk in enumerate((k_hi, k_lo)):
                        last = nc.tensor.matmul(psum[:, 4 + 2 * (un % 2) + a // HALF, 0:z - a],
                                                qs[:, h, i * P:(i + 1) * P], kk[:, a:z], start=(n == 0), stop=(n == 1))
                last.then_inc(s_sc, 1)

            def turn(n):
                _, i, h = HEADS[n]
                pe.wait_ge(s_exp, n + 1)
                for q in range(FIRST_GROUP[n], LAST_GROUP[n] + 1):
                    g = GROUP[q][1]
                    if q >= 2:
                        copied(pe, q - 2)
                    if q < 2:
                        pe.wait_ge(s_yconv, 2 * CC)
                    for blk in range(4 * g, min(4 * g + 4, i + 1)):
                        last = nc.tensor.transpose(psum[:, q % 2, (blk % 4) * P:(blk % 4 + 1) * P],
                                                   pr[:, n % 2, blk * P:(blk + 1) * P], ident)
                    last.then_inc(s_pt, 1)

            def values(n):
                _, i, h = HEADS[n]
                copied(pe, LAST_GROUP[n])
                if LAST_GROUP[n] > FIRST_GROUP[n]:
                    copied(pe, FIRST_GROUP[n])
                if h == 0 and i >= 2:
                    pe.wait_ge(s_ya, i - 1)
                for blk in range(i + 1):
                    last = nc.tensor.matmul(psum[:, 2 + i % 2, h * HD:(h + 1) * HD], pt[:, n % 2, blk * P:(blk + 1) * P],
                                            v[:, blk, :], start=(blk == 0), stop=(blk == i))
                last.then_inc(s_pv, 1)

            def turn_output(i):
                pe.wait_ge(s_o, i + 1)
                for c in range(CC):
                    last = nc.tensor.transpose(psum[:, 2 + i % 2, c * P:(c + 1) * P], o_sb[:, c * P:(c + 1) * P], ident)
                last.then_inc(s_ot, 1)

            def output(un, i):
                free_ring(un)
                pe.wait_ge(s_ylo, i + 1)
                pe.wait_ge(s_wos, KC)
                for n2 in range(2):
                    for k in range(KC):
                        for n, (y, w) in enumerate(((yt_hi, wo_hi), (yt_hi, wo_lo), (yt_lo, wo_hi))):
                            last = nc.tensor.matmul(psum[:, 4 + 2 * (un % 2) + n2, :], y[:, k, :],
                                                    w[:, k, n2 * HALF:(n2 + 1) * HALF],
                                                    start=(k == 0 and n == 0), stop=(k == KC - 1 and n == 2))
                last.then_inc(s_op, 1)

            n = 0
            for un, unit in enumerate(UNITS):
                if unit[0] == "h":
                    scores(un, unit[1], unit[2])
                    if n >= 1:
                        turn(n - 1)
                    if n >= 2:
                        values(n - 2)
                    if unit[2] == 2 and unit[1] >= 1:
                        turn_output(unit[1] - 1)
                    n += 1
                    if n == len(HEADS):
                        turn(n - 1)
                        values(n - 2)
                        values(n - 1)
                        turn_output(TT - 1)
                else:
                    output(un, unit[1])

        def ring(a, n):
            return psum[:, a:a + 2, :].rearrange("p a b -> p (a b)")[:, 0:n]

        @block.scalar
        def _(act):
            act.wait_ge(s_tables, 64)
            nc.scalar.activation(c_th, col("c", 0, KC), ACT.Tanh, scale=0.5).then_inc(s_cth, 1)
            for i in range(TT):
                act.wait_ge(s_x[i], 16)
                if i >= 1:
                    act.wait_ge(s_ss, i)
                nc.scalar.activation(x_sq[:], xin[:, i, :], ACT.Square, accum_out=ss[:, i:i + 1]).then_inc(s_ss, 1)
            act.wait_ge(s_g1, 1)
            for t in range(16):
                half, k = t // KC, t % KC
                act.wait_ge(s_xt, t + 1)
                if t >= 4:
                    act.wait_ge(s_hlo, t - 3)
                nc.scalar.activation(h32[:, t % 4, :], psum[:, t % 4, :], ACT.Identity, bias=mod[:, k:k + 1],
                                     scale=g1[:, k:k + 1]).then_inc(s_h32, 1)

            def bank(b):
                c, half = BANKS[b]
                kind = CHUNKS[c]
                src = psum[:, b % 4, :]
                sl = slice(half * HALF, (half + 1) * HALF)
                if kind[0] == "A":
                    return
                act.wait_ge(s_proj, b + 1)
                if kind == "KI":
                    nc.scalar.copy(ki_raw[:, sl], src).then_inc(s_raw, 1)
                elif kind == "KV":
                    nc.scalar.copy(kv_raw[:, sl], src).then_inc(s_raw, 1)
                elif kind[:2] == "QI":
                    m = 2 * int(kind[2]) + half
                    if m >= 2:
                        act.wait_ge(s_qst[m % 2], 64)
                    nc.scalar.copy(t_hi[:, m % 2, :], src).then_inc(s_thi, 1)
                elif kind[0] == "Q":
                    j = int(kind[1])
                    nc.scalar.activation(q_raw[:, j, sl], src, ACT.Identity, scale=con("qscale", j, 1)).then_inc(s_q, 1)
                elif kind[:2] in ("GA", "GC"):
                    dst = (ga if kind[1] == "A" else gc)[:, int(kind[2]), sl]
                    if b - GATES >= 1:
                        act.wait_ge(s_silu, b - GATES)
                    if kind == "GC0" and half == 0:
                        for g in range(2):
                            act.wait_ge(s_cnt[g], ROUNDS)
                        act.wait_ge(s_klo, 1)
                        act.wait_ge(s_vt, 1)
                    nc.scalar.activation(dst, src, ACT.Copy, scale=0.5)
                    nc.scalar.activation(tg[:], src, ACT.Tanh, scale=0.5).then_inc(s_gat, 1)
                else:
                    m = 2 * int(kind[1]) + half
                    if m >= 1:
                        act.wait_ge(s_u, m)
                    nc.scalar.activation(th[:], src, ACT.Tanh, scale=0.5).then_inc(s_tanh, 1)

            bank(0)
            bank(1)
            act.wait_ge(s_raw, 2)
            nc.scalar.copy(ki_hi[0:HD, :], ki_raw[0:HD, :]).then_inc(s_kihi, 1)
            for b in range(2, EARLY):
                bank(b)
            act.wait_ge(s_wit, 1)
            nc.scalar.copy(wi.rearrange("p (t h) -> p t h", t=TT),
                           ring(4, T).rearrange("p (t c) -> p t c", t=TT)[:, :, HD:HD + NI]).then_inc(s_wi, 1)
            for e, (i, j) in enumerate(IDX):
                act.wait_ge(s_idx, e + 1)
                if e >= 2:
                    act.wait_ge(s_acc, e - 1)
                nc.scalar.activation(rl[:, e % 2, 0:keys(i)], ring(4 + 2 * (e % 2), keys(i)), ACT.Relu)\
                    .then_inc(s_relu, 1)
            for n in range(ROUNDS):
                for g in range(2):
                    act.wait_ge(s_cand[g], n + 1)
                    for i in GROUPS[g]:
                        o = off(i) - off(FIRST)
                        last = nc.scalar.activation(junk[:, o:o + keys(i)], xs[:, off(i):off(i) + keys(i)], ACT.Sign,
                                                    bias=cand_f[:, COL[i]:COL[i] + 1], scale=-1.0,
                                                    accum_out=sums[:, COL[i]:COL[i] + 1])
                    last.then_inc(s_cnt[g], 1)
                    if g == 0 and EARLY + n < DURING:
                        bank(EARLY + n)
                if n == 7:
                    act.wait_ge(s_raw, 4)
                    nc.scalar.copy(k_hi[0:HD, :], kv_raw[0:HD, :]).then_inc(s_khi, 1)
                if n == 10:
                    act.wait_ge(s_vt, 1)
                    nc.scalar.copy(v[:], ring(4, T).rearrange("p (t c) -> p t c", t=TT)[:, :, HD:P]).then_inc(s_v, 1)
            for b in range(DURING, DURING + 4):
                bank(b)

            def square(half):
                for c in range(CC):
                    m = CC * half + c
                    act.wait_ge(s_yc, m + 1)
                    if m >= 2:
                        act.wait_ge(s_var, m - 1)
                    nc.scalar.activation(sq[:, m % 2, :], yc[:, c, half * HALF:(half + 1) * HALF], ACT.Square)\
                        .then_inc(s_sq, 1)

            square(0)
            bank(44)
            bank(45)
            square(1)
            bank(46)
            bank(47)
            act.wait_ge(s_var, 2 * CC)
            for half in range(2):
                nc.scalar.activation(rstd[:, half, :], psum[:, 6 + half, :], ACT.Sqrt, bias=con("eps"))\
                    .then_inc(s_std, 1)

            def z_high(m):
                half, c = m // CC, m % CC
                sl = slice(half * HALF, (half + 1) * HALF)
                act.wait_ge(s_zs, m + 1)
                if m == 0:
                    act.wait_ge(s_proj, 2 * NCH)
                nc.scalar.copy(z_hi[:, c, sl], yc[:, c, sl]).then_inc(s_zhi, 1)

            for m in range(2 * CC):
                half, c = m // CC, m % CC
                sl = slice(half * HALF, (half + 1) * HALF)
                act.wait_ge(s_yn, m + 1)
                if m >= 2:
                    act.wait_ge(s_zs, m - 1)
                nc.scalar.activation(zt[:, m % 2, :], yc[:, c, sl], ACT.Tanh, bias=col("b_cn", c), scale=col("g_cn", c))
                nc.scalar.activation(zz[:, m % 2, :], yc[:, c, sl], ACT.Identity, bias=col("b_cn", c),
                                     scale=col("g_cn", c)).then_inc(s_zt, 1)
                if m >= 1:
                    z_high(m - 1)
            z_high(2 * CC - 1)
            for j in range(CC):
                act.wait_ge(s_q, 2 * CC)
                nc.scalar.copy(qs[0:HD, 2 * j, :], q_raw[0:HD, j, :])
                nc.scalar.copy(qs[HD:P, 2 * j + 1, :], q_raw[HD:P, j, :]).then_inc(s_qhi, 1)
            act.wait_ge(s_gb, 1)
            act.wait_ge(s_bias, TT)
            nc.scalar.copy(gate[:], ring(4, D)).then_inc(s_gate, 1)

            def copy_groups(n):
                for q in range(FIRST_GROUP[n], LAST_GROUP[n] + 1):
                    if OWNER[q] != 0:
                        continue
                    g = GROUP[q][1]
                    w = min(HALF, keys(HEADS[n][1]) - g * HALF)
                    act.wait_ge(s_pt, q + 1)
                    if n >= 2:
                        act.wait_ge(s_pv, n - 1)
                    nc.scalar.copy(pt[:, n % 2, g * HALF:g * HALF + w], psum[:, q % 2, 0:w]).then_inc(s_pe0[0], 1)

            def y_high(i):
                sl = slice(i * P, (i + 1) * P)
                act.wait_ge(s_ya, i + 1)
                if i == 0:
                    act.wait_ge(s_wos, KC)
                    act.wait_ge(s_yconv, 2 * CC)
                else:
                    act.wait_ge(s_op, i)
                nc.scalar.copy(yt_hi[:, 0:CC, :], ga[:, :, sl])
                nc.scalar.copy(yt_hi[:, CC:2 * CC, :], gc[:, :, sl]).then_inc(s_yhi, 1)

            def out_square(i):
                act.wait_ge(s_op, i + 1)
                if i >= 1:
                    act.wait_ge(s_osq, i)
                un = UNITS.index(("o", i))
                nc.scalar.activation(sq_junk[:], ring(4 + 2 * (un % 2), D), ACT.Square, accum_out=osq[:, i:i + 1])\
                    .then_inc(s_osq, 1)

            for n, (_, i, h) in enumerate(HEADS):
                act.wait_ge(s_mx, n + 1)
                if n >= 2:
                    act.wait_ge(s_pt, LAST_GROUP[n - 2] + 1)
                nc.scalar.activation(pr[:, n % 2, 0:keys(i)], sm[:, n % 2, 0:keys(i)], ACT.Exp,
                                     bias=nb[:, n % 2:n % 2 + 1], scale=2.0 ** -(h + 1),
                                     accum_out=denom[:, NH * (i % 2) + h:NH * (i % 2) + h + 1]).then_inc(s_exp, 1)
                if n >= 1:
                    copy_groups(n - 1)
                if h == 3 and i >= 1:
                    y_high(i - 1)
                if h == 4 and i >= 1:
                    out_square(i - 1)
            copy_groups(len(HEADS) - 1)
            y_high(TT - 1)
            out_square(TT - 1)

        @block.vector
        def _(dve):
            link_n = [0]

            def link(ins):
                link_n[0] += 1
                ins.then_inc(s_dve, 1)
                dve.wait_ge(s_dve, link_n[0])

            nc.vector.memset(pw, -0.5)
            nc.vector.memset(u[:, :, 0:PAD], 0.0)
            link(nc.vector.memset(cand_f, 0.0))
            dve.wait_ge(s_tables, 64)
            for name in ("w_dw", "g_cn", "b_cn"):
                w = COLS[name][1]
                link(nc.vector.tensor_scalar(col(name, 0, w), col(name, 0, w), 0.5, None, ALU.mult))
            dve.wait_ge(s_cth, 1)
            link(nc.vector.scalar_tensor_tensor(out=c_act, in0=c_th, scalar=1.0, in1=col("c", 0, KC), op0=ALU.add,
                                                op1=ALU.mult))
            nc.vector.tensor_scalar(c_act, c_act, 0.5, None, ALU.mult).then_inc(s_cact, 1)
            for i in range(TT):
                if i % 4 == 0:
                    dve.wait_ge(s_rx, i // 4 + 1)
                nc.vector.tensor_scalar(xin[:, i, :], xin[:, i, :], rx[:, i:i + 1], None, ALU.mult).then_inc(s_xn, 1)
            dve.wait_ge(s_mod, 8)
            link(nc.vector.tensor_tensor(mod[:, 0:2 * KC], psum[:, 7, 0:2 * KC], col("b_ada", 0, 2 * KC), ALU.add))
            nc.vector.scalar_tensor_tensor(out=g1, in0=mod[:, KC:2 * KC], scalar=1.0, in1=col("g_pre", 0, KC),
                                           op0=ALU.add, op1=ALU.mult).then_inc(s_g1, 1)
            for t in range(16):
                dve.wait_ge(s_h32, t + 1)
                nc.vector.tensor_copy(h_hi[:, t % KC, (t // KC) * HALF:(t // KC + 1) * HALF], h32[:, t % 4, :])\
                    .then_inc(s_hhi, 1)
            dve.wait_ge(s_kihi, 1)
            nc.vector.tensor_tensor(ki_lo[0:HD, :], ki_raw[0:HD, :], ki_hi[0:HD, :], ALU.subtract).then_inc(s_kilo, 1)
            dve.wait_ge(s_mod, 12)
            gs = slice(2 * KC, 3 * KC)
            link(nc.vector.tensor_tensor(mod[:, gs], psum[:, 7, gs], col("b_ada", 2 * KC, KC), ALU.add))
            nc.vector.scalar_tensor_tensor(out=mod[:, gs], in0=mod[:, gs], scalar=float(HALF), in1=col("g_post", 0, KC),
                                           op0=ALU.mult, op1=ALU.mult).then_inc(s_g1, 1)

            def bank(b):
                c, half = BANKS[b]
                kind = CHUNKS[c]
                if kind[:2] == "QI":
                    m = 2 * int(kind[2]) + half
                    dve.wait_ge(s_thi, m + 1)
                    nc.vector.tensor_tensor(t_lo[:, m % 2, :], psum[:, b % 4, :], t_hi[:, m % 2, :], ALU.subtract)\
                        .then_inc(s_tlo, 1)
                elif kind[0] == "A":
                    p = int(kind[1])
                    dve.wait_ge(s_proj, b + 1)
                    dve.wait_ge(s_tanh, 2 * p + half + 1)
                    nc.vector.scalar_tensor_tensor(
                        out=u[:, p % 2, PAD + half * HALF:PAD + (half + 1) * HALF], in0=th[:], scalar=1.0,
                        in1=psum[:, b % 4, :], op0=ALU.add, op1=ALU.mult).then_inc(s_u, 1)

            for b in range(2, EARLY):
                bank(b)
            dve.wait_ge(s_wi, 1)
            for e, (i, j) in enumerate(IDX):
                dve.wait_ge(s_relu, e + 1)
                dst = xs[:, off(i):off(i) + keys(i)]
                r, w = rl[:, e % 2, 0:keys(i)], wi[:, NI * i + j:NI * i + j + 1]
                if j == 0:
                    nc.vector.tensor_scalar(dst, r, w, None, ALU.mult).then_inc(s_acc, 1)
                else:
                    dve.wait_ge(s_acc, e)
                    nc.vector.scalar_tensor_tensor(out=dst, in0=r, scalar=w, in1=dst, op0=ALU.mult, op1=ALU.add)\
                        .then_inc(s_acc, 1)

            taps = [0]

            def tap(c, k):
                src, w = u[:, c % 2, k:k + T], col("w_dw", TAPS * c + k)
                if k == 0:
                    dve.wait_ge(s_u, 2 * (c + 1))
                    ins = nc.vector.tensor_scalar(yc[:, c, :], src, w, col("b_dw", c), ALU.mult, ALU.add)
                else:
                    dve.wait_ge(s_y, TAPS * c + k)
                    ins = nc.vector.scalar_tensor_tensor(out=yc[:, c, :], in0=src, scalar=w, in1=yc[:, c, :],
                                                         op0=ALU.mult, op1=ALU.add)
                ins.then_inc(s_y, 1)

            def span(g):
                return slice(3 * g, 3 * g + 3)

            def update(n, g):
                dve.wait_ge(s_cnt[g], n + 1)
                link(nc.vector.tensor_tensor(cond[:, span(g)], sums[:, span(g)], con("few", 3 * g, 3), ALU.is_le))
                link(nc.vector.copy_predicated(found[:, span(g)], cond[:, span(g)], cand[:, span(g)]))
                if n + 1 < ROUNDS:
                    nc.vector.tensor_scalar(cand[:, span(g)], found[:, span(g)], bits[:, n + 1:n + 2], None,
                                            ALU.bitwise_xor).then_inc(s_cand[g], 1)

            dve.wait_ge(s_caus, TT - FIRST)
            for g in range(2):
                nc.vector.tensor_scalar(found[:, span(g)], cand[:, span(g)], bits[:, 0:1], None,
                                        ALU.bitwise_xor).then_inc(s_cand[g], 1)
            for n in range(ROUNDS):
                c, k = n // 8, 4 * (n % 8)
                tap(c, k)
                update(n, 0)
                tap(c, k + 1)
                if EARLY + n < DURING:
                    bank(EARLY + n)
                tap(c, k + 2)
                update(n, 1)
                if k + 3 < TAPS:
                    tap(c, k + 3)
                if n == 8:
                    dve.wait_ge(s_khi, 1)
                    nc.vector.tensor_tensor(k_lo[0:HD, :], kv_raw[0:HD, :], k_hi[0:HD, :], ALU.subtract)\
                        .then_inc(s_klo, 1)
            for m in range(2 * CC):
                half, c = m // CC, m % CC
                sl = slice(half * HALF, (half + 1) * HALF)
                dve.wait_ge(s_mu, half + 1)
                nc.vector.tensor_tensor(yc[:, c, sl], yc[:, c, sl], psum[:, 4 + half, :], ALU.subtract)\
                    .then_inc(s_yc, 1)
            for half in range(2):
                dve.wait_ge(s_std, half + 1)
                link(nc.vector.reciprocal(rstd[:, half, :], rstd[:, half, :]))
                for c in range(CC):
                    sl = slice(half * HALF, (half + 1) * HALF)
                    dve.wait_ge(s_yc, CC * half + c + 1)
                    nc.vector.tensor_tensor(yc[:, c, sl], yc[:, c, sl], rstd[:, half, :], ALU.mult).then_inc(s_yn, 1)

            def z_low(m):
                half, c = m // CC, m % CC
                sl = slice(half * HALF, (half + 1) * HALF)
                dve.wait_ge(s_zhi, m + 1)
                nc.vector.tensor_tensor(z_lo[:, c, sl], yc[:, c, sl], z_hi[:, c, sl], ALU.subtract).then_inc(s_zlo, 1)

            for m in range(2 * CC):
                half, c = m // CC, m % CC
                dve.wait_ge(s_zt, m + 1)
                nc.vector.scalar_tensor_tensor(out=yc[:, c, half * HALF:(half + 1) * HALF], in0=zt[:, m % 2, :],
                                               scalar=1.0, in1=zz[:, m % 2, :], op0=ALU.add, op1=ALU.mult)\
                    .then_inc(s_zs, 1)
                if m >= 1:
                    z_low(m - 1)
            z_low(2 * CC - 1)
            for k in range(KC):
                ins = nc.vector.tensor_scalar(diag[:, k, :], con("ident"), mod[:, 2 * KC + k:2 * KC + k + 1], None,
                                              ALU.mult)
            ins.then_inc(s_diag, 1)
            for j in range(CC):
                dve.wait_ge(s_qhi, j + 1)
                nc.vector.tensor_tensor(q_lo[0:HD, j, :], q_raw[0:HD, j, :], qs[0:HD, 2 * j, :], ALU.subtract)
                nc.vector.tensor_tensor(q_lo[HD:P, j, :], q_raw[HD:P, j, :], qs[HD:P, 2 * j + 1, :], ALU.subtract)\
                    .then_inc(s_qlo, 1)
            for m in range(CC):
                for half in range(2):
                    b = 2 * NCH + 2 * m + half
                    sl = slice(half * HALF, (half + 1) * HALF)
                    dve.wait_ge(s_proj, b + 1)
                    dve.wait_ge(s_silu, 16)
                    nc.vector.scalar_tensor_tensor(out=gc[:, m, sl], in0=psum[:, b % 4, :], scalar=col("b_pw2", m),
                                                   in1=gc[:, m, sl], op0=ALU.add, op1=ALU.mult).then_inc(s_yconv, 1)

            def count_above(dst):
                for i in ORDER:
                    a, n = COL[i], keys(i)
                    ins = nc.vector.tensor_scalar(run[:, 0:n], xs[:, off(i):off(i) + n], found_f[:, a:a + 1], None,
                                                  ALU.is_gt, ALU.add, accum_out=dst[:, a:a + 1])
                    link(ins)

            link(nc.vector.tensor_scalar(itmp, found, 0x7F800000, None, ALU.bitwise_and))
            link(nc.vector.tensor_scalar(f_tmp, itmp, 0.0, None, ALU.is_gt))
            link(nc.vector.tensor_tensor(found_f, found_f, f_tmp, ALU.mult))
            count_above(above)
            link(nc.vector.tensor_scalar(f_tmp, found_f, 0.0, 2.0, ALU.is_ge, ALU.mult))
            link(nc.vector.tensor_scalar(cand, f_tmp, -1.0, None, ALU.add))
            link(nc.vector.tensor_tensor(cand, found, cand, ALU.add))
            link(nc.vector.tensor_scalar(cond, above, float(TOPK), None, ALU.is_ge))
            link(nc.vector.copy_predicated(found, cond, cand))
            count_above(above)
            link(nc.vector.tensor_scalar(above, above, -1.0, float(TOPK), ALU.mult, ALU.add))
            for n, i in enumerate(range(FIRST, TT)):
                a, w = COL[i], keys(i)
                xi, t, r = xs[:, off(i):off(i) + w], tie[:, 0:w], run[:, 0:w]
                if n >= 1:
                    dve.wait_ge(s_bias, FIRST + n)
                link(nc.vector.tensor_scalar(t, xi, found_f[:, a:a + 1], None, ALU.is_equal))
                link(nc.vector.tensor_tensor_scan(r, t, t, 0.0, ALU.add, ALU.max))
                link(nc.vector.scalar_tensor_tensor(out=t, in0=r, scalar=above[:, a:a + 1], in1=t, op0=ALU.is_le,
                                                    op1=ALU.mult))
                nc.vector.scalar_tensor_tensor(out=t, in0=xi, scalar=found_f[:, a:a + 1], in1=t, op0=ALU.is_gt,
                                               op1=ALU.add).then_inc(s_sel, 1)

            def copy_groups(n):
                for q in range(FIRST_GROUP[n], LAST_GROUP[n] + 1):
                    if OWNER[q] != 1:
                        continue
                    g = GROUP[q][1]
                    w = min(HALF, keys(HEADS[n][1]) - g * HALF)
                    dve.wait_ge(s_pt, q + 1)
                    if n >= 2:
                        dve.wait_ge(s_pv, n - 1)
                    nc.vector.tensor_copy(pt[:, n % 2, g * HALF:g * HALF + w], psum[:, q % 2, 0:w])\
                        .then_inc(s_pe0[1], 1)

            def normalise(i):
                dve.wait_ge(s_exp, NH * (i + 1))
                link(nc.vector.reciprocal(rden, denom[:, NH * (i % 2):NH * (i % 2 + 1)]))
                dve.wait_ge(s_pv, NH * (i + 1))
                if i >= 1:
                    dve.wait_ge(s_ot, i)
                nc.vector.tensor_tensor(o_sb[:].rearrange("p (h d) -> p h d", h=NH),
                                        psum[:, 2 + i % 2, :].rearrange("p (h d) -> p h d", h=NH),
                                        rden.rearrange("p (h a) -> p h a", a=1).broadcast_to([P, NH, HD]), ALU.mult)\
                    .then_inc(s_o, 1)

            def gate_attention(i):
                dve.wait_ge(s_ot, i + 1)
                dve.wait_ge(s_silu, 16)
                dst = ga[:, :, i * P:(i + 1) * P]
                nc.vector.tensor_tensor(dst, psum[:, 2 + i % 2, :].rearrange("p (c t) -> p c t", c=CC), dst, ALU.mult)\
                    .then_inc(s_ya, 1)

            def y_low(i):
                sl = slice(i * P, (i + 1) * P)
                dve.wait_ge(s_yhi, i + 1)
                nc.vector.tensor_tensor(yt_lo[:, 0:CC, :], ga[:, :, sl], yt_hi[:, 0:CC, :], ALU.subtract)
                nc.vector.tensor_tensor(yt_lo[:, CC:2 * CC, :], gc[:, :, sl], yt_hi[:, CC:2 * CC, :], ALU.subtract)\
                    .then_inc(s_ylo, 1)

            def finish(i):
                un = UNITS.index(("o", i))
                r = ring(4 + 2 * (un % 2), D)
                dve.wait_ge(s_or, i + 1)
                link(nc.vector.scalar_tensor_tensor(out=r, in0=r, scalar=orr[:, i:i + 1], in1=gate[:], op0=ALU.mult,
                                                    op1=ALU.mult))
                dve.wait_ge(s_xo[i % 2], 16 * (i // 2 + 1))
                nc.vector.tensor_tensor(xo[:, i % 2, :], r, xo[:, i % 2, :], ALU.add).then_inc(s_of, 1)

            dve.wait_ge(s_bias, TT)
            for n, (_, i, h) in enumerate(HEADS):
                un = UNITS.index(("h", i, h))
                dve.wait_ge(s_sc, n + 1)
                if n >= 2:
                    dve.wait_ge(s_exp, n - 1)
                link(nc.vector.tensor_tensor_reduce(
                    out=sm[:, n % 2, 0:keys(i)], in0=ring(4 + 2 * (un % 2), keys(i)),
                    in1=xs[:, off(i):off(i) + keys(i)], scale=1.0, scalar=3.0 * NEG, op0=ALU.add, op1=ALU.max,
                    accum_out=mx[:, n % 2:n % 2 + 1]))
                nc.vector.tensor_scalar(nb[:, n % 2:n % 2 + 1], mx[:, n % 2:n % 2 + 1], -2.0 ** -(h + 1), None,
                                        ALU.mult).then_inc(s_mx, 1)
                if n >= 1:
                    copy_groups(n - 1)
                if i >= 1:
                    if h == 1:
                        normalise(i - 1)
                    if h == 2:
                        gate_attention(i - 1)
                    if h == 3:
                        y_low(i - 1)
                    if h == 4:
                        finish(i - 1)
            copy_groups(len(HEADS) - 1)
            normalise(TT - 1)
            gate_attention(TT - 1)
            y_low(TT - 1)
            finish(TT - 1)

        @block.gpsimd
        def _(pool):
            link_n = [0]

            def link(ins):
                link_n[0] += 1
                ins.then_inc(s_pool, 1)
                pool.wait_ge(s_pool, link_n[0])

            def rstd_of(dst, squares):
                link(nc.gpsimd.tensor_scalar(ms[:, 0:dst.shape[1]], squares, 1.0 / D, EPS, ALU.mult, ALU.add))
                return nc.gpsimd.tensor_tensor(dst, ms[:, 0:dst.shape[1]], pw[:, 0:dst.shape[1]], ALU.pow)

            def split(c):
                pool.wait_ge(s_w[c % 2], 16 * (c // 2 + 1))
                if c >= 2:
                    pool.wait_ge(s_proj, LAST_OF[c - 2] + 1 if c - 2 < NCH else 2 * (c - 2) + 2)
                n = KC if c < NCH else CC
                link(nc.gpsimd.tensor_copy(w_hi[:, c % 2, 0:n, :], w_raw[:, c % 2, 0:n, :]))
                nc.gpsimd.tensor_tensor(w_lo[:, c % 2, 0:n, :], w_raw[:, c % 2, 0:n, :], w_hi[:, c % 2, 0:n, :],
                                        ALU.subtract).then_inc(s_split, 1)

            def silu(b):
                c, half = BANKS[b]
                dst = (ga if CHUNKS[c][1] == "A" else gc)[:, int(CHUNKS[c][2]), half * HALF:(half + 1) * HALF]
                pool.wait_ge(s_gat, b - GATES + 1)
                link(nc.gpsimd.tensor_tensor(tg[:], tg[:], dst, ALU.mult))
                nc.gpsimd.tensor_tensor(dst, tg[:], dst, ALU.add).then_inc(s_silu, 1)

            for m in range(2):
                pool.wait_ge(s_ss, 4 * (m + 1))
                if m == 0:
                    pool.wait_ge(s_cact, 1)
                rstd_of(rx[:, 4 * m:4 * m + 4], ss[:, 4 * m:4 * m + 4]).then_inc(s_rx, 1)
                if m == 0:
                    pool.wait_ge(s_rx, 1)
            split(0)
            split(1)
            for t in range(16):
                pool.wait_ge(s_hhi, t + 1)
                dst = (slice(None), t % KC, slice((t // KC) * HALF, (t // KC + 1) * HALF))
                nc.gpsimd.tensor_tensor(h_lo[dst], h32[:, t % 4, :], h_hi[dst], ALU.subtract).then_inc(s_hlo, 1)
            for c in range(2, 7):
                split(c)
            for n, i in enumerate(range(FIRST, TT)):
                pool.wait_ge(s_acc, NI * (n + 1))
                a = off(i) + i * P
                nc.gpsimd.affine_select(out=xs[:, a:a + P], in_=xs[:, a:a + P], compare_op=ALU.is_ge, fill=NEG,
                                        base=0, pattern=[[-1, P]], channel_multiplier=1).then_inc(s_caus, 1)
            for i in range(FIRST):
                a = off(i)
                link(nc.gpsimd.tensor_copy(xs[:, a:a + keys(i)], distance[:, 7 * P - i * P:7 * P - i * P + keys(i)]))
                nc.gpsimd.affine_select(out=xs[:, a + i * P:a + keys(i)], in_=xs[:, a + i * P:a + keys(i)],
                                        compare_op=ALU.is_ge, fill=NEG, base=0, pattern=[[-1, P]],
                                        channel_multiplier=1).then_inc(s_bias, 1)
            for c in range(7, NCH + CC):
                split(c)
                for b in range(GATES, 2 * NCH):
                    if BANKS[b][0] == c - 2:
                        silu(b)
            for c in range(KC):
                pool.wait_ge(s_wo[c % 2], 16 * (c // 2 + 1))
                if c == 0:
                    pool.wait_ge(s_proj, 2 * (NCH + CC))
                    pool.wait_ge(s_qs, 32 * CC)
                link(nc.gpsimd.tensor_copy(wo_hi[:, c, :], wo_raw[:, c % 2, :]))
                nc.gpsimd.tensor_tensor(wo_lo[:, c, :], wo_raw[:, c % 2, :], wo_hi[:, c, :], ALU.subtract)\
                    .then_inc(s_wos, 1)
            for n, i in enumerate(range(FIRST, TT)):
                w = keys(i)
                xi = xs[:, off(i):off(i) + w]
                pool.wait_ge(s_sel, n + 1)
                link(nc.gpsimd.tensor_scalar(xi, tie[:, 0:w], -1.0, -NEG, ALU.add, ALU.mult))
                nc.gpsimd.tensor_tensor(xi, xi, distance[:, 7 * P - i * P:7 * P - i * P + w], ALU.add)\
                    .then_inc(s_bias, 1)
            for i in range(TT):
                pool.wait_ge(s_osq, i + 1)
                rstd_of(orr[:, i:i + 1], osq[:, i:i + 1]).then_inc(s_or, 1)
                pool.wait_ge(s_or, i + 1)


_OUT = (1, T, D)


def tables():
    import numpy as np

    cons = np.zeros((P, NCONS), np.float32)

    def put(name, value):
        a, w = CONS[name]
        cons[:, a:a + w] = value

    put("ident", np.eye(P))
    put("mean", 1.0 / (CC * P))
    put("few", np.array([[keys(i) - 2.0 * TOPK for i in ORDER]]))
    put("eps", EPS)
    p = np.arange(P)[:, None]
    put("qscale", 2.0 ** (2 * np.arange(CC)[None, :] + (p >= HD) + 1) * HD ** -0.5)
    bits = [0xFFFFFFFF] + [1 << (31 - n) for n in range(1, ROUNDS)] + [0]
    masks = np.tile(np.array(bits, np.uint32).view(np.int32), (P, 1))
    dist = (np.arange(RW)[None, :] - p - 7 * P).astype(np.float16)
    return cons, masks, dist


def kernel(**inputs):
    import numpy as np
    import concourse.bacc as bacc
    from concourse import mybir as _mybir
    from concourse.bass_utils import run_bass_kernel_spmd

    a = {k: np.asarray(v) for k, v in inputs.items()}

    def column(v, n):
        return v.reshape(n, P).T

    w_dw = a["w_dw"][0].T.reshape(CC, P, TAPS).transpose(1, 0, 2).reshape(P, CC * TAPS)
    cols = np.concatenate([
        column(a["c"][0], KC), column(a["b_ada"][0], 3 * KC), column(a["g_pre"][0], KC), column(a["g_post"][0], KC),
        w_dw, column(a["b_dw"][0], CC), column(a["g_cnorm"][0], CC), column(a["b_cnorm"][0], CC),
        column(a["b_pw2"][0], CC)], axis=1)
    w_ada = a["w_ada"][0].reshape(KC, P, 12, 256).transpose(2, 1, 0, 3)
    w = a["w_in"][0]
    widths = (512, 64, 64, 512, 256, 64, 4, 1024, 512)
    q, k, v, g_att, q_i, k_i, w_i, glu, g_conv = np.split(w, np.cumsum(widths)[:-1], axis=1)
    parts = {"KI": np.concatenate([k_i, w_i, np.zeros((D, HD - NI), w.dtype)], axis=1),
             "KV": np.concatenate([k, v], axis=1)}
    for name, block in (("Q", q), ("QI", q_i), ("A", glu[:, :512]), ("G", glu[:, 512:]), ("GA", g_att),
                        ("GC", g_conv)):
        for j in range(block.shape[1] // P):
            parts[f"{name}{j}"] = block[:, j * P:(j + 1) * P]
    w_in = np.stack([parts[n].reshape(KC, P, P).transpose(1, 0, 2) for n in CHUNKS])
    w_pw2 = a["w_pw2"][0].reshape(CC, P, CC, P).transpose(2, 1, 0, 3)
    cons, masks, dist = tables()
    arrays, args = {}, []
    nc = bacc.Bacc("TRN2", target_bir_lowering=False, num_devices=1)
    for name, value in (("x", a["x"][0]), ("cols", cols), ("consts", cons), ("masks", masks), ("dist", dist), ("w_ada", w_ada),
                        ("w_in", w_in), ("w_pw2", w_pw2), ("w_out", a["w_out"][0])):
        value = np.ascontiguousarray(value)
        arrays[f"in_{name}"] = value
        args.append(nc.dram_tensor(f"in_{name}", value.shape, _mybir.dt.from_np(value.dtype), kind="ExternalInput").ap())
    res = nc.dram_tensor("out_0", (T, D), _mybir.dt.float32, kind="ExternalOutput").ap()
    hybrid_block(nc, *args, res)
    r = run_bass_kernel_spmd(nc, [arrays], core_ids=[0])
    return r.results[0]["out_0"].reshape(_OUT)
```

```python
from contextlib import ExitStack

import concourse.bass as bass
from concourse import mybir

ALU = mybir.AluOpType
ACT = mybir.ActivationFunctionType
F32 = mybir.dt.float32
F32R = mybir.dt.float32r
F16 = mybir.dt.float16
BF16 = mybir.dt.bfloat16
I32 = mybir.dt.int32

P = 128
T = 1024
D = 1024
TT = T // P
KC = D // P
HALF = 512
HD = 64
NH = 8
NI = 4
TOPK = 256
TAPS = 31
PAD = TAPS - 1
CC = 4
EPS = 1e-6
NEG = -1e30
FIRST = TOPK // P

CHUNKS = ["KI", "QI0", "QI1", "G0", "A0", "G1", "A1", "KV", "Q0", "Q1", "G2", "A2", "Q2",
          "Q3", "G3", "A3", "GA0", "GA1", "GA2", "GA3", "GC1", "GC2", "GC3", "GC0"]
AT = {name: n for n, name in enumerate(CHUNKS)}
NCH = len(CHUNKS)


def bank_plan():
    out, n = [], 0
    while n < NCH:
        if CHUNKS[n][0] == "G" and CHUNKS[n][1].isdigit():
            out += [(n, 0), (n + 1, 0), (n, 1), (n + 1, 1)]
            n += 2
        elif n == 0:
            out += [(0, 0), (1, 0), (0, 1), (1, 1)]
            n += 2
        else:
            out += [(n, 0), (n, 1)]
            n += 1
    return out


BANKS = bank_plan()
PW2_ORDER = (0, 2, 1, 3)
ADA = [0, 2, 1, 3, 4, 5]
EARLY = 10
DURING = 42
BY_ACT = (1, 2, 3, 4)
GATES = 32
LAST_OF = {c: max(b for b, (x, _) in enumerate(BANKS) if x == c) for c in range(NCH)}
BANK_OF = {x: b for b, x in enumerate(BANKS)}

GROUPS = [(2, 3, 7), (4, 5, 6)]
ORDER = [i for g in GROUPS for i in g]
COL = {i: n for n, i in enumerate(ORDER)}
ROUNDS = 32


def keys(i):
    return (i + 1) * P


def off(i):
    return P * i * (i + 1) // 2


NSMALL = 192
XW = off(TT)
RW = T + 7 * P

COLS, _n = {}, 0
for _name, _w in (("c", KC), ("b_ada", 3 * KC), ("g_pre", KC), ("g_post", KC), ("w_dw", CC * TAPS), ("b_dw", CC),
                  ("g_cn", CC), ("b_cn", CC), ("b_pw2", CC)):
    COLS[_name] = (_n, _w)
    _n += _w
NCOLS = _n
CONS, _n = {}, 0
for _name, _w in (("ident", P), ("mean", P), ("qscale", CC), ("few", 6), ("eps", 1)):
    CONS[_name] = (_n, _w)
    _n += _w
NCONS = _n


def hybrid_block(nc, x, cols, consts, masks, dist, w_ada, w_in, w_pw2, w_out, out):
    with ExitStack() as ctx:
        nc_base = 16512
        top = 229344

        def at(name, kb, shape, dt=F32):
            size = 1
            for s in shape[1:]:
                size *= s
            size *= 2 if dt in (F16, BF16) else 4
            assert nc_base + kb + size <= top, (name, kb, size)
            return nc.alloc_sbuf_tensor_at(name, shape, dt, offset=nc_base + kb)

        K = 1024
        oH, oW = 0, 64 * K
        oY, oQ = oW + 24 * K, oW + 40 * K
        oGA = oQ + 16 * K
        oX = oGA + 16 * K
        oKI = oX + 4 * XW
        oQI = oKI + 8 * K
        oU = oQI + 16 * K
        oR = oU + (8 * (PAD + T) + 31) // 32 * 32
        oV = oR + 4 * K
        oM = oV + 2 * K
        oC = oM + (4 * (NCOLS + 8 + NSMALL) + 31) // 32 * 32
        oT = oC + (4 * (NCONS + ROUNDS + 9) + 31) // 32 * 32
        h_hi = at("h_hi", oH, [P, KC, T], F32R)
        h_lo = at("h_lo", oH + 32 * K, [P, KC, T], F32R)
        z_hi = at("z_hi", oH, [P, CC, T], F32R)
        z_lo = at("z_lo", oH + 16 * K, [P, CC, T], F32R)
        qs = at("qs", oH + 32 * K, [P, NH, T], F32R)
        wo_hi = at("wo_hi", oH, [P, KC, D], F32R)
        wo_lo = at("wo_lo", oY, [P, KC, D], F32R)
        wo_raw = at("wo_raw", oY, [P, KC, D])
        w_raw = at("w_raw", oW, [P, 2, KC, P])
        w_hi = at("w_hi", oW + 8 * K, [P, 2, KC, P], F32R)
        w_lo = at("w_lo", oW + 16 * K, [P, 2, KC, P], F32R)
        pr = at("pr", oW, [P, 4, T])
        pt = at("pt", oW + 16 * K, [P, 2, T])
        ada = at("ada", oY, [P, 4, KC // 2, HALF])
        rl = at("rl", oY, [P, 2, T])
        yc = at("yc", oY, [P, CC, T])
        q_raw = at("q_raw", oQ, [P, CC, T])
        ga = at("ga", oGA, [P, CC, T])
        xin = at("xin", oX, [P, TT, D])
        xs = at("xs", oX, [P, XW])
        ki_hi = at("ki_hi", oKI, [P, T], F32R)
        ki_lo = at("ki_lo", oKI + 4 * K, [P, T], F32R)
        k_hi = at("k_hi", oKI, [P, T], F32R)
        k_lo = at("k_lo", oKI + 4 * K, [P, T], F32R)
        qi = at("qi", oQI, [P, NI, T], F32R)
        junk_2 = at("junk_2", oQI, [P, keys(2)], BF16)
        junk = at("junk", oT, [P, XW - off(FIRST + 1)], BF16)
        kv_raw = at("kv_raw", oQI + 8448, [P, T])
        gc = at("gc", oQI, [P, CC, T])
        ki_raw = at("ki_raw", oGA + 8 * K, [P, T])
        h32 = at("h32", oGA, [P, 4, HALF])
        part = at("part", oGA + 12 * K, [P, 2, HALF])
        u = at("u", oU, [P, 2, PAD + T])
        zt = at("zt", oU, [P, 2, HALF])
        counted = at("counted", oU + 4 * K, [P, T], F16)
        tie = at("tie", oT + 4 * K, [P, T], F16)
        run = at("run", oT + 6 * K, [P, T], F16)
        yt_hi = at("yt_hi", oU, [P, 2 * CC, P], F32R)
        yt_lo = at("yt_lo", oU + 4 * K, [P, 2 * CC, P], F32R)
        distance = at("distance", oR, [P, RW], F16)
        gate = at("gate", oR, [P, D])
        v = at("v", oV, [P, TT, HD])
        colt = at("colt", oM, [P, NCOLS])
        small = at("small", oM + (4 * NCOLS + 31) // 32 * 32, [P, NSMALL])
        cons = at("cons", oC, [P, NCONS])
        bits = at("bits", oC + (4 * NCONS + 31) // 32 * 32, [P, ROUNDS + 1], I32)
        t_hi = at("t_hi", oT, [P, 2, HALF], F32R)
        t_lo = at("t_lo", oT + 4 * K, [P, 2, HALF], F32R)
        c_rep = at("c_rep", oT + 8 * K, [P, KC, P])
        picked = at("picked", oV, [P, CC, P])
        sq = at("sq", oT, [P, 2, HALF])
        rstd = at("rstd", oT + 4 * K, [P, 2, HALF])
        diag = at("diag", oT, [P, KC, P])
        xo = at("xo", oT, [P, 2, D])
        th = at("th", oT + 8 * K, [P, HALF])
        tg = at("tg", oT + 10 * K, [P, HALF])
        o_sb = at("o_sb", oT + 8 * K, [P, CC * P])
        sq_junk = at("sq_junk", oT + 10 * K, [P, D], BF16)
        q_lo = at("q_lo", oQ, [P, CC, T], F32R)
        x_sq = at("x_sq", oU + 4 * K + 256, [P, D])

        psum = ctx.enter_context(nc.psum_tensor("psum", [P, 8, HALF], F32))

        _c = {}

        def col(name, j=0, n=1):
            a, w = COLS[name]
            return colt[:, a + j:a + j + n]

        def con(name, j=0, n=None):
            a, w = CONS[name]
            return cons[:, a + j:a + (w if n is None else j + n)]

        used = [0]

        def scratch(n):
            used[0] += n
            assert used[0] <= NSMALL
            return small[:, used[0] - n:used[0]]

        ss, ms, rx, pw = scratch(TT), scratch(TT), scratch(TT), scratch(TT)
        c_th, c_act, c_512 = scratch(KC), scratch(KC), scratch(KC)
        mod, g1 = scratch(3 * KC), scratch(KC)
        found_f, cand_f, sums, cond_f, f_tmp = scratch(6), scratch(6), scratch(6), scratch(6), scratch(6)
        found, cand, cond, itmp = (a.bitcast(I32) for a in (found_f, cand_f, cond_f, f_tmp))
        above = scratch(6)
        wi = scratch(TT * NI)
        mx, nb = scratch(2), scratch(2)
        denom = scratch(2 * NH)
        rden = scratch(NH)

        def sem(name):
            return ctx.enter_context(nc.semaphore(name))

        s_tables = sem("tables_loaded")
        s_x = [sem(f"x_loaded_{i}") for i in range(TT)]
        s_ada = [sem(f"ada_loaded_{i}") for i in range(4)]
        s_w = [sem(f"w_loaded_{i}") for i in range(2)]
        s_pw2 = [sem(f"pw2_loaded_{i}") for i in range(CC)]
        s_dup = sem("ki_doubled")
        s_kdup = sem("k_doubled")
        s_qst = [sem(f"qi_stacked_{i}") for i in range(2)]
        s_qs = sem("q_stacked")
        s_wo = [sem(f"wo_loaded_{i}") for i in range(KC)]
        s_xo = [sem(f"x_again_{i}") for i in range(2)]
        s_out = [sem(f"out_stored_{i}") for i in range(2)]
        s_cth = sem("c_tanh_done")
        s_cact = sem("c_act_done")
        s_ss = sem("x_squares_done")
        s_rx = sem("x_rstd_done")
        s_xn = sem("x_normed")
        s_pool = sem("pool_chain")
        s_dve = sem("dve_chain")
        s_mod = sem("ada_half_multiplied")
        s_part = sem("ada_half_weighted")
        s_row = sem("mod_rows_done")
        s_g1 = sem("mod_ready")
        s_xt = sem("x_transposed")
        s_h32 = sem("h32_ready")
        s_hhi = sem("h_hi_ready")
        s_hlo = [sem("h_lo_ready_even"), sem("h_lo_ready_odd")]
        s_split = sem("w_split")
        s_wh = sem("w_hi_by_act")
        s_proj = sem("proj_bank_done")
        s_raw = sem("raw_evacuated")
        s_kihi = sem("ki_hi_ready")
        s_kilo = sem("ki_lo_ready")
        s_thi = sem("t_hi_ready")
        s_tlo = sem("t_lo_ready")
        s_tanh = sem("tanh_ready")
        s_u = sem("u_half_ready")
        s_wit = sem("wi_transposed")
        s_wi = sem("wi_ready")
        s_idx = sem("index_logits_done")
        s_relu = sem("relu_done")
        s_acc = sem("index_score_added")
        s_caus = sem("causal_filled")
        s_cand = [sem(f"candidates_ready_{g}") for g in range(2)]
        s_cnt = [sem(f"counts_ready_{g}") for g in range(2)]
        s_gat = sem("gate_tanh_ready")
        s_silu = sem("gate_silu_ready")
        s_vt = sem("v_transposed")
        s_v = sem("v_ready")
        s_khi = sem("k_hi_ready")
        s_klo = sem("k_lo_ready")
        s_q = sem("q_raw_ready")
        s_y = sem("conv_done")
        s_mu = sem("mean_done")
        s_yc = sem("centred")
        s_sq = sem("square_done")
        s_var = sem("variance_done")
        s_std = sem("std_ready")
        s_yn = sem("normed")
        s_zt = sem("z_affine_tanh_ready")
        s_zs = sem("z_silu_ready")
        s_zhi = sem("z_hi_ready")
        s_zlo = sem("z_lo_ready")
        s_yconv = sem("conv_branch_ready")
        s_qhi = sem("q_hi_ready")
        s_qlo = [sem("q_lo_by_dve"), sem("q_lo_by_pool")]
        s_sel = sem("selection_ready")
        s_masked = sem("mask_scaled")
        s_bias = sem("bias_ready")
        s_diag = sem("gate_diagonal_ready")
        s_gb = sem("gate_broadcast")
        s_gate = sem("gate_rows_ready")
        s_wos = sem("wo_split")
        s_woh = sem("wo_hi_ready")
        s_sc = sem("scores_done")
        s_mx = sem("row_max_ready")
        s_exp = sem("probs_ready")
        s_pt = sem("probs_transposed")
        s_ptc = [sem("pt_copied_by_act"), sem("pt_copied_by_dve")]
        s_pv = sem("pv_done")
        s_o = sem("o_normalised")
        s_ot = sem("o_transposed")
        s_ya = sem("y_att_ready")
        s_yhi = [sem("y_conv_hi_ready"), sem("y_att_hi_ready")]
        s_ylo = [sem("y_conv_lo_ready"), sem("y_att_lo_ready")]
        s_opc = sem("out_product_half_done")
        s_op = sem("out_product_done")
        s_osq = sem("out_squares_done")
        s_or = sem("out_rstd_ready")
        s_og = sem("out_gated")
        s_of = sem("out_tile_ready")

        osq, orr = ss, rx

        def gate_tanh(b):
            return th if b >= DURING and b % 2 == 0 else tg

        def rows_pw2(m):
            return slice(CC * (m // 2), CC * (m // 2) + CC)

        def emptied(eng, b):
            if b < 0:
                eng.wait_ge(s_h32, KC + b + 1)
                return
            if b >= 2 * NCH:
                eng.wait_ge(s_yconv, b - 2 * NCH + 1)
                return
            kind = CHUNKS[BANKS[b][0]]
            same = [x for x in range(b + 1) if CHUNKS[BANKS[x][0]].rstrip("0123456789") == kind.rstrip("0123456789")]
            if kind == "KI":
                eng.wait_ge(s_raw, len(same))
            elif kind == "KV":
                eng.wait_ge(s_raw, 2 + len(same))
            elif kind[:2] == "QI":
                eng.wait_ge(s_tlo, len(same))
            elif kind[0] == "Q":
                eng.wait_ge(s_q, len(same))
            elif kind[:2] in ("GA", "GC"):
                eng.wait_ge(s_gat, b - GATES + 1)
            elif kind[0] == "G":
                eng.wait_ge(s_tanh, len(same))
            else:
                eng.wait_ge(s_u, len(same))

        IDX = [(i, j) for i in range(FIRST, TT) for j in range(NI)]
        HEADS = [(i, h) for i in range(TT) for h in range(NH)]
        NU = len(HEADS)
        STEPS = NU + 4

        def groups(n):
            return range((HEADS[n][0] + 4) // 4)

        PT_USES = []
        for step in range(STEPS):
            if 2 <= step < NU + 2:
                PT_USES += [("p", step - 2, g) for g in groups(step - 2)]
            if step % NH == 3 and step > NH:
                PT_USES.append(("o", step // NH - 1))
        OWNER = {}
        DONE_BY = {}
        _by = [0, 0]
        for use in PT_USES:
            if use[0] == "p":
                _, n, g = use
                o = g if len(groups(n)) == 2 else n % 2
                _by[o] += 1
                OWNER[n, g], DONE_BY[n, g] = o, _by[o]
        TURNED = {use[1:]: q + 1 for q, use in enumerate([x for x in PT_USES if x[0] == "p"])}
        PARTS = 3
        PIECES = {step: [] for step in range(STEPS)}
        for _j in range(TT - 1):
            for _p in range(PARTS):
                PIECES[NH * (_j + 1) + 5 + _p].append((_j, False, _p, PARTS))
                PIECES[NH * (_j + 1) + 8 + _p].append((_j, True, _p, PARTS))
        PIECES[NU + 2].append((TT - 1, False, 0, 3))
        PIECES[NU + 3].append((TT - 1, False, 1, 3))

        def out_bank(i):
            return 4 if i == TT - 1 else BANK_OUT

        LAST_GATES = {0: 44, 1: 45, 3: 46, 4: 47}
        GATE_STEP = 12
        SELECT_STEPS = {0: 2, 2: 3, 4: 4, 6: 5, 8: 6, 10: 7}
        BANK_PT, BANK_O, BANK_OUT = 2, 3, 0

        def copied(eng, n, g):
            eng.wait_ge(s_ptc[OWNER[n, g]], DONE_BY[n, g])

        def ada_bank(m):
            return 4 + m % 4 if m < 4 else m + 2

        block = ctx.enter_context(nc.Block())

        def words(a):
            return a.bitcast(F32)

        @block.sync
        def _(sp):
            def store(i):
                sp.wait_ge(s_of, i + 1)
                sp.dma_start(out[i * P:(i + 1) * P, :], xo[:, i % 2, :]).then_inc(s_out[i % 2], 16)

            sp.dma_start(cons[:], consts).then_inc(s_tables, 16)
            sp.dma_start(bits[:], masks).then_inc(s_tables, 16)
            sp.dma_start(colt[:], cols).then_inc(s_tables, 16)
            sp.dma_start(distance[:], dist).then_inc(s_tables, 16)

            def load_x(half):
                for i in range(4 * half, 4 * half + 4):
                    sp.dma_start(xin[:, i, :], x[i * P:(i + 1) * P, :]).then_inc(s_x[i], 16)

            def load_ada(b):
                if b >= 4:
                    sp.wait_ge(s_mod, b - 3)
                    sp.wait_ge(s_part, b - 3)
                sp.dma_start(ada[:, b % 4], w_ada[b]).then_inc(s_ada[b % 4], 16)

            def load_w(c):
                if c >= 2:
                    sp.wait_ge(s_split, c - 1)
                sp.dma_start(w_raw[:, c % 2], w_in[c]).then_inc(s_w[c % 2], 16)

            def load_pw2(m):
                if m < 2:
                    sp.wait_ge(s_split, NCH + m - 1)
                sp.dma_start(w_raw[:, m % 2, rows_pw2(m), :], w_pw2[m]).then_inc(s_pw2[m], 16)

            def stack_qi(m):
                c, half, s = m // 2, m % 2, m % 2
                sl = slice(half * HALF, (half + 1) * HALF)
                sp.wait_ge(s_tlo, m + 1)
                for head, a in ((2 * c, 0), (2 * c + 1, HD)):
                    sp.dma_start(words(qi[0:HD, head, sl]), words(t_hi[a:a + HD, s, :])).then_inc(s_qst[s], 16)
                    sp.dma_start(words(qi[HD:P, head, sl]), words(t_lo[a:a + HD, s, :])).then_inc(s_qst[s], 16)

            load_x(0)
            load_ada(0)
            load_ada(1)
            load_w(0)
            for b in range(2, 8):
                load_ada(b)
            load_w(1)
            load_x(1)
            for b in range(8, 12):
                load_ada(b)
            load_w(2)
            load_w(3)
            sp.wait_ge(s_kilo, 1)
            sp.dma_start(words(ki_hi[HD:P, :]), words(ki_hi[0:HD, :])).then_inc(s_dup, 16)
            sp.dma_start(words(ki_lo[HD:P, :]), words(ki_lo[0:HD, :])).then_inc(s_dup, 16)
            stack_qi(0)
            stack_qi(1)
            load_w(4)
            stack_qi(2)
            stack_qi(3)
            for c in range(5, 16):
                load_w(c)
            sp.wait_ge(s_klo, 1)
            sp.dma_start(words(k_hi[HD:P, :]), words(k_hi[0:HD, :])).then_inc(s_kdup, 16)
            sp.dma_start(words(k_lo[HD:P, :]), words(k_lo[0:HD, :])).then_inc(s_kdup, 16)
            for c in range(16, NCH):
                load_w(c)
            for m in PW2_ORDER:
                load_pw2(m)
            for j in (0, 1, 2, 3):
                sp.wait_ge(s_qlo[j // 2], j % 2 + 1)
                sp.dma_start(words(qs[HD:P, 2 * j, :]), words(q_lo[0:HD, j, :])).then_inc(s_qs, 16)
                sp.dma_start(words(qs[0:HD, 2 * j + 1, :]), words(q_lo[HD:P, j, :])).then_inc(s_qs, 16)
            sp.wait_ge(s_zlo, 2 * CC)
            for c in range(KC):
                if c == CC:
                    sp.wait_ge(s_qs, 32 * CC)
                sp.dma_start(wo_raw[:, c, :], w_out[c * P:(c + 1) * P, :]).then_inc(s_wo[c], 16)
            sp.wait_ge(s_gb, 1)
            for i in range(TT):
                if i == 1:
                    sp.wait_ge(s_sel, TT - FIRST)
                if i >= 2:
                    sp.wait_ge(s_out[i % 2], 16 * (i // 2))
                sp.dma_start(xo[:, i % 2, :], x[i * P:(i + 1) * P, :]).then_inc(s_xo[i % 2], 16)
                if i >= 1:
                    store(i - 1)
            store(TT - 1)
            for k in range(2):
                sp.wait_ge(s_out[k], 16 * (TT // 2))

        @block.tensor
        def _(pe):
            ident = con("ident")

            def ada_half(b):
                m = b // 2
                pe.wait_ge(s_ada[b % 4], 16 * (b // 4 + 1))
                for k in range(CC // 2):
                    last = nc.tensor.matmul(psum[:, ada_bank(m), :], c_rep[:, CC * (b % 2) + k, :], ada[:, b % 4, k, :],
                                            start=(b % 2 == 0 and k == 0), stop=False)
                last.then_inc(s_mod, 1)

            def ada_rest(m):
                pe.wait_ge(s_part, 2 * (m + 1))
                nc.tensor.matmul(psum[:, ada_bank(m), :], con("mean"), part[:, m % 2, :], start=(m >= 4), stop=True)\
                    .then_inc(s_row, 1)

            def turn_x(t):
                half, k = t // KC, t % KC
                pe.wait_ge(s_xn, 4 * (half + 1))
                if KC <= t < KC + 4:
                    pe.wait_ge(s_g1, 2)
                elif t >= 4:
                    pe.wait_ge(s_h32, t - 3)
                for j in range(4):
                    last = nc.tensor.transpose(psum[:, 4 * half + t % 4, j * P:(j + 1) * P],
                                               xin[:, 4 * half + j, k * P:(k + 1) * P], ident)
                last.then_inc(s_xt, 1)

            pe.wait_ge(s_cact, 1)
            for m in range(4):
                ada_half(2 * m)
                ada_half(2 * m + 1)
                ada_rest(m)
                if m == 1:
                    for t in range(4):
                        turn_x(t)
            for t in range(4, KC):
                turn_x(t)

            def project(b):
                c, half = BANKS[b]
                sl = slice(half * HALF, (half + 1) * HALF)
                emptied(pe, b - 4)
                pe.wait_ge(s_split, c + 1)
                if b in (0, 2):
                    for p in range(2):
                        pe.wait_ge(s_hlo[p], CC * (half + 1))
                for k in range(KC):
                    for n, (w, h) in enumerate(((w_hi, h_hi), (w_hi, h_lo), (w_lo, h_hi))):
                        last = nc.tensor.matmul(psum[:, b % 4, :], w[:, c % 2, k, :], h[:, k, sl],
                                                start=(k == 0 and n == 0), stop=(k == KC - 1 and n == 2))
                last.then_inc(s_proj, 1)

            project(0)
            for t in range(KC, 12):
                turn_x(t)
            project(1)
            for t in range(12, 16):
                turn_x(t)
            for b in range(2, 6):
                project(b)
            ada_rest(4)
            ada_rest(5)
            pe.wait_ge(s_raw, 2)
            pe.wait_ge(s_g1, 3)
            for i in range(TT):
                last = nc.tensor.transpose(psum[:, 4 + i // 4, (i % 4) * P:(i % 4 + 1) * P],
                                           ki_raw[:, i * P:(i + 1) * P], ident)
            last.then_inc(s_wit, 1)
            project(6)
            pe.wait_ge(s_dup, 32)
            for k in range(2):
                pe.wait_ge(s_qst[k], 128)
            for e, (i, j) in enumerate(IDX):
                if e == 0:
                    pe.wait_ge(s_wi, 1)
                if e >= 2:
                    pe.wait_ge(s_relu, e - 1)
                for a in range(0, keys(i), HALF):
                    z = min(a + HALF, keys(i))
                    for n, kk in enumerate((ki_hi, ki_lo)):
                        last = nc.tensor.matmul(psum[:, 4 + 2 * (e % 2) + a // HALF, 0:z - a],
                                                qi[:, j, i * P:(i + 1) * P], kk[:, a:z],
                                                start=(n == 0), stop=(n == 1))
                last.then_inc(s_idx, 1)
                if e in (4, 11, 18):
                    project(7 + e // 7)
            for b in range(EARLY, 18):
                project(b)
            pe.wait_ge(s_raw, 4)
            pe.wait_ge(s_relu, len(IDX))
            for i in range(TT):
                last = nc.tensor.transpose(psum[:, 4 + i // 4, (i % 4) * P:(i % 4 + 1) * P],
                                           kv_raw[:, i * P:(i + 1) * P], ident)
            last.then_inc(s_vt, 1)

            def mean(c):
                pe.wait_ge(s_y, TAPS * (c + 1))
                if c == 0:
                    pe.wait_ge(s_v, 1)
                for half in range(2):
                    last = nc.tensor.matmul(psum[:, 4 + half, :], con("mean"),
                                            yc[:, c, half * HALF:(half + 1) * HALF], start=(c == 0), stop=(c == CC - 1))
                    if c == CC - 1:
                        last.then_inc(s_mu, 1)

            def variance(half):
                for c in range(CC):
                    m = CC * half + c
                    pe.wait_ge(s_sq, m + 1)
                    nc.tensor.matmul(psum[:, 6 + half, :], con("mean"), sq[:, m % 2, :],
                                     start=(c == 0), stop=(c == CC - 1)).then_inc(s_var, 1)

            for b in range(18, 2 * NCH - 2):
                project(b)
                if b in (26, 32, 40):
                    mean((b - 25) // 7)
            mean(CC - 1)
            variance(0)
            variance(1)
            project(46)
            project(47)
            for half in range(2):
                pe.wait_ge(s_zlo, CC * (half + 1))
                for n_chunk, m in enumerate(PW2_ORDER):
                    b = 2 * NCH + CC * half + n_chunk
                    emptied(pe, b - 4)
                    pe.wait_ge(s_split, NCH + n_chunk + 1)
                    rows = rows_pw2(m)
                    for k in range(CC):
                        for n, (w, z) in enumerate(((w_hi, z_hi), (w_hi, z_lo), (w_lo, z_hi))):
                            last = nc.tensor.matmul(psum[:, b % 4, :], w[:, m % 2, rows, :][:, k, :],
                                                    z[:, k, half * HALF:(half + 1) * HALF],
                                                    start=(k == 0 and n == 0), stop=(k == CC - 1 and n == 2))
                    last.then_inc(s_proj, 1)

            pe.wait_ge(s_qs, 32 * CC)
            pe.wait_ge(s_kdup, 32)
            pe.wait_ge(s_std, 2)

            def scores(n):
                i, h = HEADS[n]
                if n >= 2:
                    pe.wait_ge(s_mx, n - 1)
                for a in range(0, keys(i), HALF):
                    z = min(a + HALF, keys(i))
                    for m, kk in enumerate((k_hi, k_lo)):
                        last = nc.tensor.matmul(psum[:, 4 + 2 * (n % 2) + a // HALF, 0:z - a],
                                                qs[:, h, i * P:(i + 1) * P], kk[:, a:z], start=(m == 0), stop=(m == 1))
                last.then_inc(s_sc, 1)

            def free_pt(use):
                q = PT_USES.index(use)
                if q == 0:
                    pe.wait_ge(s_yconv, 2 * CC)
                elif PT_USES[q - 1][0] == "p":
                    copied(pe, *PT_USES[q - 1][1:])
                else:
                    pe.wait_ge(s_ya, PT_USES[q - 1][1] + 1)

            def turn(n, g):
                i, h = HEADS[n]
                pe.wait_ge(s_exp, n + 1)
                free_pt(("p", n, g))
                for blk in range(4 * g, min(4 * g + 4, i + 1)):
                    last = nc.tensor.transpose(psum[:, BANK_PT, (blk % 4) * P:(blk % 4 + 1) * P],
                                               pr[:, n % 4, blk * P:(blk + 1) * P], ident)
                last.then_inc(s_pt, 1)

            def values(n):
                i, h = HEADS[n]
                for g in groups(n):
                    copied(pe, n, g)
                if h == 0 and i >= 1:
                    pe.wait_ge(s_o, i)
                for blk in range(i + 1):
                    last = nc.tensor.matmul(psum[:, BANK_O, h * HD:(h + 1) * HD], pt[:, n % 2, blk * P:(blk + 1) * P],
                                            v[:, blk, :], start=(blk == 0), stop=(blk == i))
                last.then_inc(s_pv, 1)

            def turn_output(i):
                pe.wait_ge(s_o, i + 1)
                free_pt(("o", i))
                for c in range(CC):
                    last = nc.tensor.transpose(psum[:, BANK_PT, c * P:(c + 1) * P], o_sb[:, c * P:(c + 1) * P], ident)
                last.then_inc(s_ot, 1)

            def gate_rows():
                pe.wait_ge(s_diag, 1)
                pe.wait_ge(s_yconv, 2 * CC)
                for k in range(KC):
                    last = nc.tensor.matmul(psum[:, BANK_OUT + k // 4, (k % 4) * P:(k % 4 + 1) * P], con("mean"),
                                            diag[:, k, :], start=True, stop=True)
                last.then_inc(s_gb, 1)

            def output(i, att, p, pieces):
                if p == 0:
                    pe.wait_ge(s_ylo[att], i + 1)
                    if not att:
                        if i == 0:
                            pe.wait_ge(s_gate, 1)
                            pe.wait_ge(s_wos, KC)
                        elif i < TT - 1:
                            pe.wait_ge(s_of, i)
                        else:
                            pe.wait_ge(s_mx, NU - 1)
                todo = [(n2, k, n) for n2 in range(2) for k in range(CC) for n in range(3)]
                size = len(todo) // pieces
                for n2, k, n in todo[p * size:(p + 1) * size]:
                    y, w = ((yt_hi, wo_hi), (yt_hi, wo_lo), (yt_lo, wo_hi))[n]
                    kk = k if att else CC + k
                    last = nc.tensor.matmul(psum[:, out_bank(i) + n2, :], y[:, kk, :],
                                            w[:, kk, n2 * HALF:(n2 + 1) * HALF],
                                            start=(not att and k == 0 and n == 0), stop=(att and k == CC - 1 and n == 2))
                if p == pieces - 1:
                    last.then_inc(s_op if att else s_opc, 1)

            for step in range(STEPS):
                two = 2 <= step < NU + 2 and len(groups(step - 2)) == 2
                if not two and step < NU:
                    scores(step)
                if 2 <= step < NU + 2:
                    turn(step - 2, 0)
                if two and step < NU:
                    scores(step)
                if two:
                    turn(step - 2, 1)
                if step == GATE_STEP:
                    gate_rows()
                for piece in PIECES[step]:
                    output(*piece)
                if 3 <= step < NU + 3:
                    values(step - 3)
                if step % NH == 3 and step > NH:
                    turn_output(step // NH - 1)
            output(TT - 1, False, 2, 3)
            output(TT - 1, True, 0, 1)

        def ring(a, n):
            return psum[:, a:a + 2, :].rearrange("p a b -> p (a b)")[:, 0:n]

        @block.scalar
        def _(act):
            act.wait_ge(s_tables, 64)
            nc.scalar.activation(c_th, col("c", 0, KC), ACT.Tanh, scale=0.5).then_inc(s_cth, 1)

            def x_squares(half):
                for i in range(4 * half, 4 * half + 4):
                    act.wait_ge(s_x[i], 16)
                    if i >= 1:
                        act.wait_ge(s_ss, i)
                    nc.scalar.activation(x_sq[:], xin[:, i, :], ACT.Square, accum_out=ss[:, i:i + 1])\
                        .then_inc(s_ss, 1)

            def w_high(c):
                act.wait_ge(s_w[c % 2], 16 * (c // 2 + 1))
                if c >= 2:
                    act.wait_ge(s_proj, LAST_OF[c - 2] + 1)
                nc.scalar.copy(w_hi[:, c % 2], w_raw[:, c % 2]).then_inc(s_wh, 1)

            x_squares(0)
            for t in range(16):
                half, k = t // KC, t % KC
                if t == KC:
                    x_squares(1)
                    w_high(1)
                act.wait_ge(s_g1, 1 if t < 4 else 2)
                act.wait_ge(s_xt, t + 1)
                if t >= 4:
                    act.wait_ge(s_hlo[t % 2], t // 2 - 1)
                nc.scalar.activation(h32[:, t % 4, :], psum[:, 4 * half + t % 4, :], ACT.Identity, bias=mod[:, k:k + 1],
                                     scale=g1[:, k:k + 1]).then_inc(s_h32, 1)

            def bank(b):
                c, half = BANKS[b]
                kind = CHUNKS[c]
                src = psum[:, b % 4, :]
                sl = slice(half * HALF, (half + 1) * HALF)
                if kind[0] == "A":
                    return
                act.wait_ge(s_proj, b + 1)
                if kind == "KI":
                    nc.scalar.copy(ki_raw[:, sl], src).then_inc(s_raw, 1)
                elif kind == "KV":
                    nc.scalar.copy(kv_raw[:, sl], src).then_inc(s_raw, 1)
                elif kind[:2] == "QI":
                    m = 2 * int(kind[2]) + half
                    if m >= 2:
                        act.wait_ge(s_qst[m % 2], 64)
                    nc.scalar.copy(t_hi[:, m % 2, :], src).then_inc(s_thi, 1)
                elif kind[0] == "Q":
                    j = int(kind[1])
                    nc.scalar.activation(q_raw[:, j, sl], src, ACT.Identity, scale=con("qscale", j, 1)).then_inc(s_q, 1)
                elif kind[:2] in ("GA", "GC"):
                    dst = (ga if kind[1] == "A" else gc)[:, int(kind[2]), sl]
                    if b > DURING:
                        act.wait_ge(s_silu, b - GATES - 1)
                    elif b > GATES:
                        act.wait_ge(s_silu, b - GATES)
                    if kind == "GC0" and half == 0:
                        act.wait_ge(s_cnt[0], ROUNDS)
                    if kind == "GC1" and half == 0:
                        act.wait_ge(s_klo, 1)
                        act.wait_ge(s_vt, 1)
                    nc.scalar.activation(dst, src, ACT.Copy, scale=0.5)
                    nc.scalar.activation(gate_tanh(b)[:], src, ACT.Tanh, scale=0.5).then_inc(s_gat, 1)
                else:
                    m = 2 * int(kind[1]) + half
                    if m >= 1:
                        act.wait_ge(s_u, m)
                    nc.scalar.activation(th[:], src, ACT.Tanh, scale=0.5).then_inc(s_tanh, 1)

            for b in range(3):
                bank(b)
            w_high(2)
            act.wait_ge(s_raw, 2)
            nc.scalar.copy(ki_hi[0:HD, :], ki_raw[0:HD, :]).then_inc(s_kihi, 1)
            bank(3)
            w_high(3)
            bank(4)
            bank(5)
            w_high(4)
            act.wait_ge(s_wit, 1)
            nc.scalar.copy(wi.rearrange("p (t h) -> p t h", t=TT),
                           ring(4, T).rearrange("p (t c) -> p t c", t=TT)[:, :, HD:HD + NI]).then_inc(s_wi, 1)
            for e, (i, j) in enumerate(IDX):
                act.wait_ge(s_idx, e + 1)
                if e >= 2:
                    act.wait_ge(s_acc, e - 1)
                nc.scalar.activation(rl[:, e % 2, 0:keys(i)], ring(4 + 2 * (e % 2), keys(i)), ACT.Relu)\
                    .then_inc(s_relu, 1)
                if e in (3, 14):
                    bank(6 if e == 3 else 8)
            for n in range(ROUNDS):
                for g in range(2):
                    act.wait_ge(s_cand[g], n + 1)
                    for i in GROUPS[g]:
                        o = off(i) - off(FIRST + 1)
                        dst = junk_2[:] if i == FIRST else junk[:, o:o + keys(i)]
                        last = nc.scalar.activation(dst, xs[:, off(i):off(i) + keys(i)], ACT.Sign,
                                                    bias=cand_f[:, COL[i]:COL[i] + 1], scale=-1.0,
                                                    accum_out=sums[:, COL[i]:COL[i] + 1])
                    last.then_inc(s_cnt[g], 1)
                    if g == 0 and EARLY + n < DURING:
                        bank(EARLY + n)
                if n == 7:
                    act.wait_ge(s_raw, 4)
                    nc.scalar.copy(k_hi[0:HD, :], kv_raw[0:HD, :]).then_inc(s_khi, 1)
                if n == 10:
                    act.wait_ge(s_vt, 1)
                    nc.scalar.copy(v[:], ring(4, T).rearrange("p (t c) -> p t c", t=TT)[:, :, HD:P]).then_inc(s_v, 1)
            bank(42)
            bank(43)
            for g in range(2):
                act.wait_ge(s_cnt[g], ROUNDS)

            def square(half):
                for c in range(CC):
                    m = CC * half + c
                    act.wait_ge(s_yc, m + 1)
                    if m >= 2:
                        act.wait_ge(s_var, m - 1)
                    nc.scalar.activation(sq[:, m % 2, :], yc[:, c, half * HALF:(half + 1) * HALF], ACT.Square)\
                        .then_inc(s_sq, 1)

            square(0)
            square(1)
            for half in range(2):
                act.wait_ge(s_var, CC * (half + 1))
                nc.scalar.activation(rstd[:, half, :], psum[:, 6 + half, :], ACT.Sqrt, bias=con("eps"))\
                    .then_inc(s_std, 1)

            def q_high(j):
                act.wait_ge(s_q, 2 * CC)
                nc.scalar.copy(qs[0:HD, 2 * j, :], q_raw[0:HD, j, :])
                nc.scalar.copy(qs[HD:P, 2 * j + 1, :], q_raw[HD:P, j, :]).then_inc(s_qhi, 1)

            def z_high(m):
                half, c = m // CC, m % CC
                sl = slice(half * HALF, (half + 1) * HALF)
                act.wait_ge(s_zs, m + 1)
                if m == 0:
                    act.wait_ge(s_proj, 2 * NCH)
                nc.scalar.copy(z_hi[:, c, sl], yc[:, c, sl]).then_inc(s_zhi, 1)

            for m in range(2 * CC):
                half, c = m // CC, m % CC
                sl = slice(half * HALF, (half + 1) * HALF)
                act.wait_ge(s_yn, m + 1)
                if m >= 2:
                    act.wait_ge(s_zs, m - 1)
                nc.scalar.activation(zt[:, m % 2, :], yc[:, c, sl], ACT.Tanh).then_inc(s_zt, 1)
                if m in LAST_GATES:
                    bank(LAST_GATES[m])
                if m >= 1 and m != CC:
                    z_high(m - 1)
                if m == CC - 1:
                    z_high(m)
                    q_high(2)
                    q_high(3)
                if m in (5, 7):
                    q_high((m - 5) // 2)
            z_high(2 * CC - 1)
            def select(i):
                xi = xs[:, off(i):off(i) + keys(i)]
                act.wait_ge(s_sel, i - FIRST + 1)
                nc.scalar.activation(xi, xi, ACT.Copy, bias=NEG, scale=-NEG).then_inc(s_masked, 1)

            def copy_groups(n):
                for g in groups(n):
                    if OWNER[n, g] == 0:
                        w = min(HALF, keys(HEADS[n][0]) - g * HALF)
                        act.wait_ge(s_pt, TURNED[n, g])
                        if n >= 2:
                            act.wait_ge(s_pv, n - 1)
                        nc.scalar.copy(pt[:, n % 2, g * HALF:g * HALF + w], psum[:, BANK_PT, 0:w]).then_inc(s_ptc[0], 1)

            def y_high(i, att):
                sl = slice(i * P, (i + 1) * P)
                if att:
                    act.wait_ge(s_ya, i + 1)
                if i == 0:
                    act.wait_ge(s_zlo, 2 * CC)
                else:
                    act.wait_ge(s_op if att else s_opc, i)
                dst, src = (yt_hi[:, 0:CC, :], ga) if att else (yt_hi[:, CC:2 * CC, :], gc)
                nc.scalar.copy(dst, src[:, :, sl]).then_inc(s_yhi[att], 1)

            def out_square(i):
                act.wait_ge(s_op, i + 1)
                if i >= 1:
                    act.wait_ge(s_osq, i)
                nc.scalar.activation(sq_junk[:], ring(out_bank(i), D), ACT.Square, accum_out=osq[:, i:i + 1])\
                    .then_inc(s_osq, 1)

            for step in range(STEPS):
                if 2 <= step < NU + 2:
                    copy_groups(step - 2)
                if step < NU:
                    i, h = HEADS[step]
                    act.wait_ge(s_mx, step + 1)
                    s = pr[:, step % 4, 0:keys(i)]
                    nc.scalar.activation(s, s, ACT.Exp, bias=nb[:, step % 2:step % 2 + 1], scale=2.0 ** -(h + 1),
                                         accum_out=denom[:, NH * (i % 2) + h:NH * (i % 2) + h + 1]).then_inc(s_exp, 1)
                if step < KC:
                    if step == 0:
                        act.wait_ge(s_proj, 2 * NCH + 2 * CC)
                    act.wait_ge(s_wo[step], 16)
                    nc.scalar.copy(wo_hi[:, step, :], wo_raw[:, step, :]).then_inc(s_woh, 1)
                if step in SELECT_STEPS:
                    select(SELECT_STEPS[step])
                if step == GATE_STEP - 3:
                    for k in range(KC):
                        last = nc.scalar.mul(diag[:, k, :], con("ident"), mod[:, 2 * KC + k:2 * KC + k + 1])
                    last.then_inc(s_diag, 1)
                if step == GATE_STEP:
                    act.wait_ge(s_gb, 1)
                    act.wait_ge(s_bias, TT)
                    nc.scalar.copy(gate[:], ring(BANK_OUT, D)).then_inc(s_gate, 1)
                last_tile, h = step // NH - 1, step % NH
                if last_tile >= 0:
                    if h == 0:
                        y_high(last_tile, False)
                    if h == 2 and last_tile >= 1:
                        out_square(last_tile - 1)
                    if h == 5:
                        y_high(last_tile, True)
            y_high(TT - 1, True)
            out_square(TT - 1)

        @block.vector
        def _(dve):
            link_n = [0]

            def link(ins):
                link_n[0] += 1
                ins.then_inc(s_dve, 1)
                dve.wait_ge(s_dve, link_n[0])

            nc.vector.memset(pw, -0.5)
            nc.vector.memset(u[:, :, 0:PAD], 0.0)
            link(nc.vector.memset(cand_f, 0.0))
            dve.wait_ge(s_tables, 64)
            for name in ("w_dw", "g_cn", "b_cn"):
                w = COLS[name][1]
                link(nc.vector.tensor_scalar(col(name, 0, w), col(name, 0, w), 0.5, None, ALU.mult))
            dve.wait_ge(s_cth, 1)
            link(nc.vector.scalar_tensor_tensor(out=c_act, in0=c_th, scalar=1.0, in1=col("c", 0, KC), op0=ALU.add,
                                                op1=ALU.mult))
            nc.vector.tensor_scalar(c_512, c_act, 256.0, None, ALU.mult)
            link(nc.vector.tensor_scalar(c_act, c_act, 0.5, None, ALU.mult))
            for k in range(KC):
                ins = nc.vector.tensor_scalar(c_rep[:, k, :], con("ident"), 0.0, c_act[:, k:k + 1], ALU.mult, ALU.add)
            ins.then_inc(s_cact, 1)

            def pick(m):
                dve.wait_ge(s_row, m + 1)
                a = CC * ADA[m]
                for j in range(CC):
                    ins = nc.vector.tensor_tensor_reduce(
                        out=picked[:, j, :], in0=psum[:, ada_bank(m), j * P:(j + 1) * P], in1=con("ident"), scale=1.0,
                        scalar=0.0, op0=ALU.mult, op1=ALU.add, accum_out=mod[:, a + j:a + j + 1])
                link(ins)
                link(nc.vector.tensor_tensor(mod[:, a:a + CC], mod[:, a:a + CC], col("b_ada", a, CC), ALU.add))

            def modulation(half):
                pick(2 * half)
                pick(2 * half + 1)
                a = CC * half
                nc.vector.scalar_tensor_tensor(out=g1[:, a:a + CC], in0=mod[:, KC + a:KC + a + CC], scalar=1.0,
                                               in1=col("g_pre", a, CC), op0=ALU.add, op1=ALU.mult).then_inc(s_g1, 1)

            def weigh(b):
                m = b // 2
                dve.wait_ge(s_ada[b % 4], 16 * (b // 4 + 1))
                if b % 2 == 0 and m >= 2:
                    dve.wait_ge(s_row, m - 1)
                for k in range(0 if m >= 4 else CC // 2, CC):
                    kk = CC * (b % 2) + k
                    dst, w = part[:, m % 2, :], c_512[:, kk:kk + 1]
                    if b % 2 == 0 and k in (0, CC // 2) and not (m >= 4 and k > 0):
                        ins = nc.vector.tensor_scalar(dst, ada[:, b % 4, k, :], w, None, ALU.mult)
                    else:
                        ins = nc.vector.scalar_tensor_tensor(out=dst, in0=ada[:, b % 4, k, :], scalar=w, in1=dst,
                                                             op0=ALU.mult, op1=ALU.add)
                    if k < CC - 1:
                        link(ins)
                ins.then_inc(s_part, 1)
                dve.wait_ge(s_part, b + 1)

            def norm_x(half):
                dve.wait_ge(s_rx, half + 1)
                for i in range(4 * half, 4 * half + 4):
                    nc.vector.tensor_scalar(xin[:, i, :], xin[:, i, :], rx[:, i:i + 1], None, ALU.mult)\
                        .then_inc(s_xn, 1)

            weigh(0)
            norm_x(0)
            for b in range(1, 4):
                weigh(b)
            modulation(0)
            weigh(4)
            weigh(5)

            def h_parts(t):
                dst = (slice(None), t % KC, slice((t // KC) * HALF, (t // KC + 1) * HALF))
                dve.wait_ge(s_h32, t + 1)
                nc.vector.tensor_copy(h_hi[dst], h32[:, t % 4, :]).then_inc(s_hhi, 1)
                if t % 2:
                    dve.wait_ge(s_hhi, t + 1)
                    nc.vector.tensor_tensor(h_lo[dst], h32[:, t % 4, :], h_hi[dst], ALU.subtract).then_inc(s_hlo[1], 1)

            for t in range(4):
                h_parts(t)
            weigh(6)
            weigh(7)
            modulation(1)
            for t in range(4, KC):
                h_parts(t)
            norm_x(1)
            for t in range(KC, 16):
                h_parts(t)
            bank_1 = BANK_OF[AT["QI0"], 0]

            def bank(b):
                c, half = BANKS[b]
                kind = CHUNKS[c]
                if kind[:2] == "QI":
                    m = 2 * int(kind[2]) + half
                    dve.wait_ge(s_thi, m + 1)
                    nc.vector.tensor_tensor(t_lo[:, m % 2, :], psum[:, b % 4, :], t_hi[:, m % 2, :], ALU.subtract)\
                        .then_inc(s_tlo, 1)
                elif kind[0] == "A":
                    p = int(kind[1])
                    dve.wait_ge(s_proj, b + 1)
                    dve.wait_ge(s_tanh, 2 * p + half + 1)
                    nc.vector.scalar_tensor_tensor(
                        out=u[:, p % 2, PAD + half * HALF:PAD + (half + 1) * HALF], in0=th[:], scalar=1.0,
                        in1=psum[:, b % 4, :], op0=ALU.add, op1=ALU.mult).then_inc(s_u, 1)

            bank(bank_1)
            for b in range(8, 12):
                weigh(b)
            dve.wait_ge(s_kihi, 1)
            nc.vector.tensor_tensor(ki_lo[0:HD, :], ki_raw[0:HD, :], ki_hi[0:HD, :], ALU.subtract).then_inc(s_kilo, 1)
            for b in range(bank_1 + 1, 6):
                bank(b)
            pick(4)
            pick(5)
            gs = slice(2 * KC, 3 * KC)
            nc.vector.scalar_tensor_tensor(out=mod[:, gs], in0=mod[:, gs], scalar=float(HALF), in1=col("g_post", 0, KC),
                                           op0=ALU.mult, op1=ALU.mult).then_inc(s_g1, 1)
            dve.wait_ge(s_wi, 1)
            for e, (i, j) in enumerate(IDX):
                dve.wait_ge(s_relu, e + 1)
                dst = xs[:, off(i):off(i) + keys(i)]
                r, w = rl[:, e % 2, 0:keys(i)], wi[:, NI * i + j:NI * i + j + 1]
                if j == 0:
                    nc.vector.tensor_scalar(dst, r, w, None, ALU.mult).then_inc(s_acc, 1)
                else:
                    dve.wait_ge(s_acc, e)
                    nc.vector.scalar_tensor_tensor(out=dst, in0=r, scalar=w, in1=dst, op0=ALU.mult, op1=ALU.add)\
                        .then_inc(s_acc, 1)
                if e in (9, 21):
                    bank(7 if e == 9 else 9)

            taps = [0]

            def tap(c, k):
                src, w = u[:, c % 2, k:k + T], col("w_dw", TAPS * c + k)
                if k == 0:
                    dve.wait_ge(s_u, 2 * (c + 1))
                    ins = nc.vector.tensor_scalar(yc[:, c, :], src, w, col("b_dw", c), ALU.mult, ALU.add)
                else:
                    dve.wait_ge(s_y, TAPS * c + k)
                    ins = nc.vector.scalar_tensor_tensor(out=yc[:, c, :], in0=src, scalar=w, in1=yc[:, c, :],
                                                         op0=ALU.mult, op1=ALU.add)
                ins.then_inc(s_y, 1)

            def span(g):
                return slice(3 * g, 3 * g + 3)

            def update(n, g):
                dve.wait_ge(s_cnt[g], n + 1)
                link(nc.vector.tensor_tensor(cond[:, span(g)], sums[:, span(g)], con("few", 3 * g, 3), ALU.is_le))
                link(nc.vector.copy_predicated(found[:, span(g)], cond[:, span(g)], cand[:, span(g)]))
                if n + 1 < ROUNDS:
                    nc.vector.tensor_scalar(cand[:, span(g)], found[:, span(g)], bits[:, n + 1:n + 2], None,
                                            ALU.bitwise_xor).then_inc(s_cand[g], 1)

            dve.wait_ge(s_caus, TT - FIRST)
            for g in range(2):
                nc.vector.tensor_scalar(found[:, span(g)], cand[:, span(g)], bits[:, 0:1], None,
                                        ALU.bitwise_xor).then_inc(s_cand[g], 1)
            for n in range(ROUNDS):
                c, k = n // 8, 4 * (n % 8)
                tap(c, k)
                update(n, 0)
                tap(c, k + 1)
                if EARLY + n < DURING:
                    bank(EARLY + n)
                tap(c, k + 2)
                update(n, 1)
                if k + 3 < TAPS:
                    tap(c, k + 3)
                if n == 8:
                    dve.wait_ge(s_khi, 1)
                    nc.vector.tensor_tensor(k_lo[0:HD, :], kv_raw[0:HD, :], k_hi[0:HD, :], ALU.subtract)\
                        .then_inc(s_klo, 1)
            def count_above(dst):
                for i in ORDER:
                    a, n = COL[i], keys(i)
                    ins = nc.vector.tensor_scalar(counted[:, 0:n], xs[:, off(i):off(i) + n], found_f[:, a:a + 1], None,
                                                  ALU.is_gt, ALU.add, accum_out=dst[:, a:a + 1])
                    link(ins)

            def mask(i):
                a, w = COL[i], keys(i)
                xi, t, r = xs[:, off(i):off(i) + w], tie[:, 0:w], run[:, 0:w]
                link(nc.vector.tensor_scalar(t, xi, found_f[:, a:a + 1], None, ALU.is_equal))
                link(nc.vector.tensor_tensor_scan(r, t, t, 0.0, ALU.add, ALU.max))
                link(nc.vector.scalar_tensor_tensor(out=t, in0=r, scalar=above[:, a:a + 1], in1=t, op0=ALU.is_le,
                                                    op1=ALU.mult))
                nc.vector.scalar_tensor_tensor(out=xi, in0=xi, scalar=found_f[:, a:a + 1], in1=t, op0=ALU.is_gt,
                                               op1=ALU.add).then_inc(s_sel, 1)
                dve.wait_ge(s_sel, i - FIRST + 1)

            for m in range(2 * CC):
                half, c = m // CC, m % CC
                sl = slice(half * HALF, (half + 1) * HALF)
                dve.wait_ge(s_mu, half + 1)
                nc.vector.tensor_tensor(yc[:, c, sl], yc[:, c, sl], psum[:, 4 + half, :], ALU.subtract)\
                    .then_inc(s_yc, 1)
            dve.wait_ge(s_y, CC * TAPS)
            link(nc.vector.tensor_scalar(itmp, found, 0x7F800000, None, ALU.bitwise_and))
            link(nc.vector.tensor_scalar(f_tmp, itmp, 0.0, None, ALU.is_gt))
            link(nc.vector.tensor_tensor(found_f, found_f, f_tmp, ALU.mult))
            count_above(above)
            link(nc.vector.tensor_scalar(f_tmp, found_f, 0.0, 2.0, ALU.is_ge, ALU.mult))
            link(nc.vector.tensor_scalar(cand, f_tmp, -1.0, None, ALU.add))
            link(nc.vector.tensor_tensor(cand, found, cand, ALU.add))
            link(nc.vector.tensor_scalar(cond, above, float(TOPK), None, ALU.is_ge))
            link(nc.vector.copy_predicated(found, cond, cand))
            def z_low(m):
                half, c = m // CC, m % CC
                sl = slice(half * HALF, (half + 1) * HALF)
                dve.wait_ge(s_zhi, m + 1)
                nc.vector.tensor_tensor(z_lo[:, c, sl], yc[:, c, sl], z_hi[:, c, sl], ALU.subtract).then_inc(s_zlo, 1)

            def z(m):
                half, c = m // CC, m % CC
                sl = slice(half * HALF, (half + 1) * HALF)
                dve.wait_ge(s_zt, m + 1)
                nc.vector.scalar_tensor_tensor(out=yc[:, c, sl], in0=zt[:, m % 2, :], scalar=1.0, in1=yc[:, c, sl],
                                               op0=ALU.add, op1=ALU.mult).then_inc(s_zs, 1)
                if m >= 1 and m != CC:
                    z_low(m - 1)

            for half in range(2):
                dve.wait_ge(s_std, half + 1)
                link(nc.vector.reciprocal(rstd[:, half, :], rstd[:, half, :]))
                if half == 1:
                    z_low(CC - 1)
                for c in range(CC):
                    sl = slice(half * HALF, (half + 1) * HALF)
                    dve.wait_ge(s_yc, CC * half + c + 1)
                    link(nc.vector.tensor_tensor(yc[:, c, sl], yc[:, c, sl], rstd[:, half, :], ALU.mult))
                    nc.vector.tensor_scalar(yc[:, c, sl], yc[:, c, sl], col("g_cn", c), col("b_cn", c), ALU.mult,
                                            ALU.add).then_inc(s_yn, 1)
                for c in range(CC):
                    z(CC * half + c)
            z_low(2 * CC - 1)
            def gate_convolution(half):
                for n_chunk, m in enumerate(PW2_ORDER):
                    b = 2 * NCH + CC * half + n_chunk
                    sl = slice(half * HALF, (half + 1) * HALF)
                    dve.wait_ge(s_proj, b + 1)
                    dve.wait_ge(s_silu, 16)
                    nc.vector.scalar_tensor_tensor(out=gc[:, m, sl], in0=psum[:, b % 4, :], scalar=col("b_pw2", m),
                                                   in1=gc[:, m, sl], op0=ALU.add, op1=ALU.mult).then_inc(s_yconv, 1)

            gate_convolution(0)
            for j in range(CC // 2):
                dve.wait_ge(s_qhi, CC // 2 + j + 1)
                nc.vector.tensor_tensor(q_lo[0:HD, j, :], q_raw[0:HD, j, :], qs[0:HD, 2 * j, :], ALU.subtract)
                nc.vector.tensor_tensor(q_lo[HD:P, j, :], q_raw[HD:P, j, :], qs[HD:P, 2 * j + 1, :], ALU.subtract)\
                    .then_inc(s_qlo[0], 1)
            count_above(above)
            link(nc.vector.tensor_scalar(above, above, -1.0, float(TOPK), ALU.mult, ALU.add))
            gate_convolution(1)

            def copy_groups(n):
                for g in groups(n):
                    if OWNER[n, g] == 1:
                        w = min(HALF, keys(HEADS[n][0]) - g * HALF)
                        dve.wait_ge(s_pt, TURNED[n, g])
                        if n >= 2:
                            dve.wait_ge(s_pv, n - 1)
                        nc.vector.tensor_copy(pt[:, n % 2, g * HALF:g * HALF + w], psum[:, BANK_PT, 0:w])\
                            .then_inc(s_ptc[1], 1)

            def normalise(i):
                dve.wait_ge(s_exp, NH * (i + 1))
                link(nc.vector.reciprocal(rden, denom[:, NH * (i % 2):NH * (i % 2 + 1)]))
                dve.wait_ge(s_pv, NH * (i + 1))
                if i >= 1:
                    dve.wait_ge(s_ot, i)
                nc.vector.tensor_tensor(o_sb[:].rearrange("p (h d) -> p h d", h=NH),
                                        psum[:, BANK_O, :].rearrange("p (h d) -> p h d", h=NH),
                                        rden.rearrange("p (h a) -> p h a", a=1).broadcast_to([P, NH, HD]), ALU.mult)\
                    .then_inc(s_o, 1)

            def gate_attention(i):
                dve.wait_ge(s_ot, i + 1)
                dve.wait_ge(s_silu, 16)
                dst = ga[:, :, i * P:(i + 1) * P]
                nc.vector.tensor_tensor(dst, psum[:, BANK_PT, :].rearrange("p (c t) -> p c t", c=CC), dst, ALU.mult)\
                    .then_inc(s_ya, 1)

            def y_low(i, att):
                sl = slice(i * P, (i + 1) * P)
                rows, src = (slice(0, CC), ga) if att else (slice(CC, 2 * CC), gc)
                dve.wait_ge(s_yhi[att], i + 1)
                nc.vector.tensor_tensor(yt_lo[:, rows, :], src[:, :, sl], yt_hi[:, rows, :], ALU.subtract)\
                    .then_inc(s_ylo[att], 1)

            def gate_output(i):
                dve.wait_ge(s_osq, i + 1)
                r = ring(out_bank(i), D)
                nc.vector.tensor_tensor(r, r, gate[:], ALU.mult).then_inc(s_og, 1)

            def finish(i):
                dve.wait_ge(s_og, i + 1)
                dve.wait_ge(s_or, i + 1)
                dve.wait_ge(s_xo[i % 2], 16 * (i // 2 + 1))
                nc.vector.scalar_tensor_tensor(out=xo[:, i % 2, :], in0=ring(out_bank(i), D), scalar=orr[:, i:i + 1],
                                               in1=xo[:, i % 2, :], op0=ALU.mult, op1=ALU.add).then_inc(s_of, 1)

            dve.wait_ge(s_proj, 2 * NCH + 2 * CC)
            for step in range(STEPS):
                last_tile, h = step // NH - 1, step % NH
                if last_tile >= 0:
                    if h == 4:
                        gate_attention(last_tile)
                    if h == 6:
                        y_low(last_tile, True)
                if step < NU:
                    i, h = HEADS[step]
                    dve.wait_ge(s_sc, step + 1)
                    if step >= 4:
                        dve.wait_ge(s_pt, TURNED[step - 4, groups(step - 4)[-1]])
                    if step >= 2:
                        dve.wait_ge(s_exp, step - 1)
                    if h == 0:
                        dve.wait_ge(s_bias, i + 1)
                    m = mx[:, step % 2:step % 2 + 1]
                    link(nc.vector.tensor_tensor_reduce(
                        out=pr[:, step % 4, 0:keys(i)], in0=ring(4 + 2 * (step % 2), keys(i)),
                        in1=xs[:, off(i):off(i) + keys(i)], scale=1.0, scalar=3.0 * NEG, op0=ALU.add, op1=ALU.max,
                        accum_out=m))
                    nc.vector.tensor_scalar(nb[:, step % 2:step % 2 + 1], m, -2.0 ** -(h + 1), None,
                                            ALU.mult).then_inc(s_mx, 1)
                if 2 <= step < NU + 2:
                    copy_groups(step - 2)
                if step in SELECT_STEPS:
                    mask(SELECT_STEPS[step])
                h = step % NH
                if last_tile >= 0:
                    if h == 1:
                        y_low(last_tile, False)
                    if h == 2:
                        normalise(last_tile)
                    if h == 3 and 1 <= last_tile < TT - 1:
                        gate_output(last_tile - 1)
                    if h == 4 and last_tile >= 1:
                        finish(last_tile - 1)
            gate_attention(TT - 1)
            y_low(TT - 1, True)
            for i in range(TT - 2, TT):
                gate_output(i)
                finish(i)

        @block.gpsimd
        def _(pool):
            link_n = [0]

            def link(ins):
                link_n[0] += 1
                ins.then_inc(s_pool, 1)
                pool.wait_ge(s_pool, link_n[0])

            def rstd_of(dst, squares):
                link(nc.gpsimd.tensor_scalar(ms[:, 0:dst.shape[1]], squares, 1.0 / D, EPS, ALU.mult, ALU.add))
                return nc.gpsimd.tensor_tensor(dst, ms[:, 0:dst.shape[1]], pw[:, 0:dst.shape[1]], ALU.pow)

            def split(c):
                pool.wait_ge(s_w[c % 2], 16 * (c // 2 + 1))
                if c >= 2:
                    pool.wait_ge(s_proj, LAST_OF[c - 2] + 1)
                if c in BY_ACT:
                    pool.wait_ge(s_wh, BY_ACT.index(c) + 1)
                else:
                    link(nc.gpsimd.tensor_copy(w_hi[:, c % 2], w_raw[:, c % 2]))
                nc.gpsimd.tensor_tensor(w_lo[:, c % 2], w_raw[:, c % 2], w_hi[:, c % 2], ALU.subtract)\
                    .then_inc(s_split, 1)

            def split_pw2(m):
                rows = rows_pw2(m)
                pool.wait_ge(s_pw2[m], 16)
                if m < 2:
                    pool.wait_ge(s_proj, LAST_OF[NCH - 2 + m] + 1)
                link(nc.gpsimd.tensor_copy(w_hi[:, m % 2, rows, :], w_raw[:, m % 2, rows, :]))
                nc.gpsimd.tensor_tensor(w_lo[:, m % 2, rows, :], w_raw[:, m % 2, rows, :], w_hi[:, m % 2, rows, :],
                                        ALU.subtract).then_inc(s_split, 1)

            def silu(b):
                c, half = BANKS[b]
                dst = (ga if CHUNKS[c][1] == "A" else gc)[:, int(CHUNKS[c][2]), half * HALF:(half + 1) * HALF]
                t = gate_tanh(b)
                pool.wait_ge(s_gat, b - GATES + 1)
                link(nc.gpsimd.tensor_tensor(t[:], t[:], dst, ALU.mult))
                nc.gpsimd.tensor_tensor(dst, t[:], dst, ALU.add).then_inc(s_silu, 1)

            def h_low(t):
                pool.wait_ge(s_hhi, t + 1)
                dst = (slice(None), t % KC, slice((t // KC) * HALF, (t // KC + 1) * HALF))
                nc.gpsimd.tensor_tensor(h_lo[dst], h32[:, t % 4, :], h_hi[dst], ALU.subtract).then_inc(s_hlo[0], 1)

            pool.wait_ge(s_ss, 4)
            pool.wait_ge(s_cact, 1)
            rstd_of(rx[:, 0:4], ss[:, 0:4]).then_inc(s_rx, 1)
            split(0)
            for t in range(0, KC, 2):
                h_low(t)
            pool.wait_ge(s_rx, 1)
            pool.wait_ge(s_ss, 8)
            rstd_of(rx[:, 4:8], ss[:, 4:8]).then_inc(s_rx, 1)
            split(1)
            for t in range(KC, 16, 2):
                h_low(t)
            for c in range(2, 7):
                split(c)
            for n, i in enumerate(range(FIRST, TT)):
                pool.wait_ge(s_acc, NI * (n + 1))
                a = off(i) + i * P
                nc.gpsimd.affine_select(out=xs[:, a:a + P], in_=xs[:, a:a + P], compare_op=ALU.is_ge, fill=NEG,
                                        base=0, pattern=[[-1, P]], channel_multiplier=1).then_inc(s_caus, 1)
            for i in range(FIRST):
                a = off(i)
                link(nc.gpsimd.tensor_copy(xs[:, a:a + keys(i)], distance[:, 7 * P - i * P:7 * P - i * P + keys(i)]))
                nc.gpsimd.affine_select(out=xs[:, a + i * P:a + keys(i)], in_=xs[:, a + i * P:a + keys(i)],
                                        compare_op=ALU.is_ge, fill=NEG, base=0, pattern=[[-1, P]],
                                        channel_multiplier=1).then_inc(s_bias, 1)
            def add_distance(i):
                w = keys(i)
                xi = xs[:, off(i):off(i) + w]
                pool.wait_ge(s_masked, i - FIRST + 1)
                nc.gpsimd.tensor_tensor(xi, xi, distance[:, 7 * P - i * P:7 * P - i * P + w], ALU.add)\
                    .then_inc(s_bias, 1)

            for c in range(7, NCH):
                split(c)
                for b in range(GATES, DURING):
                    if BANKS[b][0] == c - 2:
                        silu(b)
            silu(42)
            silu(43)
            split_pw2(0)
            split_pw2(2)
            silu(44)
            split_pw2(1)
            silu(45)
            split_pw2(3)
            silu(46)
            silu(47)
            pool.wait_ge(s_silu, 16)
            for j in range(CC // 2, CC):
                pool.wait_ge(s_qhi, j - CC // 2 + 1)
                link(nc.gpsimd.tensor_tensor(q_lo[0:HD, j, :], q_raw[0:HD, j, :], qs[0:HD, 2 * j, :], ALU.subtract))
                nc.gpsimd.tensor_tensor(q_lo[HD:P, j, :], q_raw[HD:P, j, :], qs[HD:P, 2 * j + 1, :],
                                        ALU.subtract).then_inc(s_qlo[1], 1)
                pool.wait_ge(s_qlo[1], j - CC // 2 + 1)
            for c in range(KC):
                pool.wait_ge(s_woh, c + 1)
                nc.gpsimd.tensor_tensor(wo_lo[:, c, :], wo_raw[:, c, :], wo_hi[:, c, :], ALU.subtract)\
                    .then_inc(s_wos, 1)
                if c in SELECT_STEPS:
                    add_distance(SELECT_STEPS[c])
            add_distance(6)
            add_distance(7)
            for i in range(TT):
                pool.wait_ge(s_osq, i + 1)
                rstd_of(orr[:, i:i + 1], osq[:, i:i + 1]).then_inc(s_or, 1)
                pool.wait_ge(s_or, i + 1)


_OUT = (1, T, D)


def tables():
    import numpy as np

    cons = np.zeros((P, NCONS), np.float32)

    def put(name, value):
        a, w = CONS[name]
        cons[:, a:a + w] = value

    put("ident", np.eye(P))
    put("mean", 1.0 / (CC * P))
    put("few", np.array([[keys(i) - 2.0 * TOPK for i in ORDER]]))
    put("eps", EPS)
    p = np.arange(P)[:, None]
    put("qscale", 2.0 ** (2 * np.arange(CC)[None, :] + (p >= HD) + 1) * HD ** -0.5)
    bits = [0xFFFFFFFF] + [1 << (31 - n) for n in range(1, ROUNDS)] + [0]
    masks = np.tile(np.array(bits, np.uint32).view(np.int32), (P, 1))
    dist = (np.arange(RW)[None, :] - p - 7 * P).astype(np.float16)
    return cons, masks, dist


def kernel(**inputs):
    import numpy as np
    import concourse.bacc as bacc
    from concourse import mybir as _mybir
    from concourse.bass_utils import run_bass_kernel_spmd

    a = {k: np.asarray(v) for k, v in inputs.items()}

    def column(v, n):
        return v.reshape(n, P).T

    w_dw = a["w_dw"][0].T.reshape(CC, P, TAPS).transpose(1, 0, 2).reshape(P, CC * TAPS)
    cols = np.concatenate([
        column(a["c"][0], KC), column(a["b_ada"][0], 3 * KC), column(a["g_pre"][0], KC), column(a["g_post"][0], KC),
        w_dw, column(a["b_dw"][0], CC), column(a["g_cnorm"][0], CC), column(a["b_cnorm"][0], CC),
        column(a["b_pw2"][0], CC)], axis=1)
    w_ada = a["w_ada"][0].reshape(2, CC, P, 6, HALF).transpose(3, 0, 2, 1, 4)[ADA].reshape(12, P, CC, HALF)
    w = a["w_in"][0]
    widths = (512, 64, 64, 512, 256, 64, 4, 1024, 512)
    q, k, v, g_att, q_i, k_i, w_i, glu, g_conv = np.split(w, np.cumsum(widths)[:-1], axis=1)
    parts = {"KI": np.concatenate([k_i, w_i, np.zeros((D, HD - NI), w.dtype)], axis=1),
             "KV": np.concatenate([k, v], axis=1)}
    for name, block in (("Q", q), ("QI", q_i), ("A", glu[:, :512]), ("G", glu[:, 512:]), ("GA", g_att),
                        ("GC", g_conv)):
        for j in range(block.shape[1] // P):
            parts[f"{name}{j}"] = block[:, j * P:(j + 1) * P]
    w_in = np.stack([parts[n].reshape(KC, P, P).transpose(1, 0, 2) for n in CHUNKS])
    w_pw2 = a["w_pw2"][0].reshape(CC, P, CC, P).transpose(2, 1, 0, 3)
    cons, masks, dist = tables()
    arrays, args = {}, []
    nc = bacc.Bacc("TRN2", target_bir_lowering=False, num_devices=1)
    for name, value in (("x", a["x"][0]), ("cols", cols), ("consts", cons), ("masks", masks), ("dist", dist), ("w_ada", w_ada),
                        ("w_in", w_in), ("w_pw2", w_pw2), ("w_out", a["w_out"][0])):
        value = np.ascontiguousarray(value)
        arrays[f"in_{name}"] = value
        args.append(nc.dram_tensor(f"in_{name}", value.shape, _mybir.dt.from_np(value.dtype), kind="ExternalInput").ap())
    res = nc.dram_tensor("out_0", (T, D), _mybir.dt.float32, kind="ExternalOutput").ap()
    hybrid_block(nc, *args, res)
    r = run_bass_kernel_spmd(nc, [arrays], core_ids=[0])
    return r.results[0]["out_0"].reshape(_OUT)
```
